# Optimizing a Trainium2 kernel written in Bass

```python
import math
import jax, jax.numpy as jnp
from jax import lax
import numpy as np

D_MODEL = 1024
BATCH = 1
SEQ = 1024
DEPTH = 1

D_MIX = D_MODEL
DA_HEADS = 4
DA_HEAD_DIM = D_MODEL // 16
DA_V_DIM = 2 * DA_HEAD_DIM
DA_WIDTH = DA_HEADS * DA_V_DIM
SB_HEADS = 8
SB_HEAD_DIM = D_MODEL // 16
SB_WIDTH = SB_HEADS * SB_HEAD_DIM
N_BUCKETS = 32
MAX_DISTANCE = 128
Q_BLOCK = 128
EPS = 1e-6
NEG_INF = -1e30

COL_SIZES = (
    DA_HEADS * 2 * DA_HEAD_DIM,
    DA_HEADS * 2 * DA_HEAD_DIM,
    DA_WIDTH,
    DA_WIDTH,
    SB_WIDTH,
    SB_WIDTH,
    SB_WIDTH,
    SB_WIDTH,
)
D_IN = sum(COL_SIZES)
COL_SPLITS = tuple(int(v) for v in np.cumsum(COL_SIZES)[:-1])

kernel_name = "hybrid_diffattn_stickbreaking_adaln"

def lambda_init_fn(layer_idx):
    return 0.8 - 0.6 * math.exp(-0.3 * layer_idx)

def rmsnorm(x, g):
    xf = x.astype(jnp.float32)
    xf = xf * lax.rsqrt(jnp.mean(xf * xf, axis=-1, keepdims=True) + EPS)
    return (xf * g.astype(jnp.float32)).astype(x.dtype)

def rel_bucket(n):
    max_exact = N_BUCKETS // 2
    nf = jnp.maximum(n, 1).astype(jnp.float32)
    large = max_exact + (jnp.log(nf / max_exact) / math.log(MAX_DISTANCE / max_exact)
                         * (N_BUCKETS - max_exact)).astype(jnp.int32)
    large = jnp.minimum(large, N_BUCKETS - 1)
    return jnp.where(n < max_exact, n, large)

def differential_attention(q, k, v, rel_bias, lam, sub_g, lambda_init):
    B, S, H, _, d = q.shape
    nb = S // Q_BLOCK
    scale = 1.0 / math.sqrt(d)
    q_blocks = q.reshape(B, nb, Q_BLOCK, H, 2, d).transpose(1, 0, 3, 4, 2, 5)
    keys = k.transpose(0, 2, 3, 1, 4)
    vals = v.transpose(0, 2, 1, 3)
    key_pos = jnp.arange(S, dtype=jnp.int32)

    def block(args):
        q_blk, start = args
        q_pos = start + jnp.arange(Q_BLOCK, dtype=jnp.int32)
        rel = q_pos[:, None] - key_pos[None, :]
        causal = rel >= 0
        bias = rel_bias[rel_bucket(jnp.maximum(rel, 0))].astype(jnp.float32)
        bias = bias.transpose(2, 0, 1)
        logits = jnp.einsum('bhmqd,bhmkd->bhmqk', q_blk, keys).astype(jnp.float32) * scale
        logits = logits + bias[None, :, None]
        logits = jnp.where(causal, logits, NEG_INF)
        p = jax.nn.softmax(logits, axis=-1)
        attn = p[:, :, 0] - lam * p[:, :, 1]
        return jnp.einsum('bhqk,bhkv->bhqv', attn.astype(vals.dtype), vals)

    starts = jnp.arange(nb, dtype=jnp.int32) * Q_BLOCK
    out = lax.map(block, (q_blocks, starts))
    out = out.transpose(1, 0, 3, 2, 4).reshape(B, S, H, -1)
    out = rmsnorm(out, sub_g) * (1.0 - lambda_init)
    return out.reshape(B, S, -1)

def stick_breaking_attention(q, k, v):
    B, S, H, d = q.shape
    nb = S // Q_BLOCK
    scale = 1.0 / math.sqrt(d)
    q_blocks = q.reshape(B, nb, Q_BLOCK, H, d).transpose(1, 0, 3, 2, 4)
    keys = k.transpose(0, 2, 1, 3)
    vals = v.transpose(0, 2, 1, 3)
    key_pos = jnp.arange(S, dtype=jnp.int32)

    def block(args):
        q_blk, start = args
        q_pos = start + jnp.arange(Q_BLOCK, dtype=jnp.int32)
        strict = key_pos[None, :] < q_pos[:, None]
        z = jnp.einsum('bhqd,bhkd->bhqk', q_blk, keys).astype(jnp.float32) * scale
        log_beta = jax.nn.log_sigmoid(z)
        log_keep = jnp.where(strict, jax.nn.log_sigmoid(-z), 0.0)
        after = lax.cumsum(log_keep, axis=3, reverse=True) - log_keep
        w = jnp.where(strict, jnp.exp(log_beta + after), 0.0)
        return jnp.einsum('bhqk,bhkv->bhqv', w.astype(vals.dtype), vals)

    starts = jnp.arange(nb, dtype=jnp.int32) * Q_BLOCK
    out = lax.map(block, (q_blocks, starts))
    return out.transpose(1, 0, 3, 2, 4).reshape(B, S, -1)

def setup_inputs(seed: int = 0) -> dict:
    key = jax.random.key(seed)
    ks = jax.random.split(key, 15)
    f32 = jnp.float32
    x = jax.random.normal(ks[0], (BATCH, SEQ, D_MODEL), f32)
    c = jax.random.normal(ks[1], (BATCH, D_MODEL), f32)
    norm_g = 1.0 + 0.05 * jax.random.normal(ks[2], (DEPTH, D_MODEL), f32)
    w_ada = 0.5 * D_MODEL ** -0.5 * jax.random.normal(ks[3], (DEPTH, D_MODEL, 3 * D_MODEL), f32)
    b_ada = 0.01 * jax.random.normal(ks[4], (DEPTH, 3 * D_MODEL), f32)
    w_in = D_MODEL ** -0.5 * jax.random.normal(ks[5], (DEPTH, D_MODEL, D_IN), f32)
    lambda_q1 = 0.1 * jax.random.normal(ks[6], (DEPTH, DA_HEAD_DIM), f32)
    lambda_k1 = 0.1 * jax.random.normal(ks[7], (DEPTH, DA_HEAD_DIM), f32)
    lambda_q2 = 0.1 * jax.random.normal(ks[8], (DEPTH, DA_HEAD_DIM), f32)
    lambda_k2 = 0.1 * jax.random.normal(ks[9], (DEPTH, DA_HEAD_DIM), f32)
    subln_g = 1.0 + 0.05 * jax.random.normal(ks[10], (DEPTH, DA_V_DIM), f32)
    w_out = D_MIX ** -0.5 * jax.random.normal(ks[11], (DEPTH, D_MIX, D_MODEL), f32)
    rel_bias = 0.5 * jax.random.normal(ks[12], (N_BUCKETS, DA_HEADS), f32)
    final_g = 1.0 + 0.05 * jax.random.normal(ks[13], (D_MODEL,), f32)
    return {"x": x, "c": c, "norm_g": norm_g, "w_ada": w_ada, "b_ada": b_ada,
            "w_in": w_in, "lambda_q1": lambda_q1, "lambda_k1": lambda_k1,
            "lambda_q2": lambda_q2, "lambda_k2": lambda_k2, "subln_g": subln_g,
            "w_out": w_out, "rel_bias": rel_bias, "final_g": final_g}

def reference(x, c, norm_g, w_ada, b_ada, w_in, lambda_q1, lambda_k1, lambda_q2, lambda_k2,
              subln_g, w_out, rel_bias, final_g):
    B, S, D = x.shape
    for l in range(DEPTH):
        lambda_init = lambda_init_fn(l)
        mod = jax.nn.silu(c) @ w_ada[l] + b_ada[l]
        shift, scl, gate = jnp.split(mod, 3, axis=-1)
        h = rmsnorm(x, norm_g[l]) * (1.0 + scl[:, None, :]) + shift[:, None, :]
        proj = h @ w_in[l]
        q_da, k_da, v_da, g_da, q_sb, k_sb, v_sb, g_sb = jnp.split(proj, COL_SPLITS, axis=-1)
        lam = (jnp.exp(jnp.sum(lambda_q1[l] * lambda_k1[l]).astype(jnp.float32))
               - jnp.exp(jnp.sum(lambda_q2[l] * lambda_k2[l]).astype(jnp.float32))
               + lambda_init)
        o_da = differential_attention(
            q_da.reshape(B, S, DA_HEADS, 2, DA_HEAD_DIM),
            k_da.reshape(B, S, DA_HEADS, 2, DA_HEAD_DIM),
            v_da.reshape(B, S, DA_HEADS, DA_V_DIM),
            rel_bias, lam, subln_g[l], lambda_init)
        o_sb = stick_breaking_attention(
            q_sb.reshape(B, S, SB_HEADS, SB_HEAD_DIM),
            k_sb.reshape(B, S, SB_HEADS, SB_HEAD_DIM),
            v_sb.reshape(B, S, SB_HEADS, SB_HEAD_DIM))
        mixed = jnp.concatenate([o_da * jax.nn.silu(g_da), o_sb * jax.nn.silu(g_sb)], axis=-1)
        y = mixed @ w_out[l]
        x = x + gate[:, None, :] * y
    return rmsnorm(x, final_g)


_drawn_inputs = setup_inputs


def setup_inputs(seed=0):
    import zlib

    import numpy as np

    out = dict(_drawn_inputs(seed))
    spreads = {}
    factors = {'norm_g': 4.919,
     'b_ada': 7.905,
     'lambda_q1': 64.0,
     'lambda_k1': 64.0,
     'lambda_q2': 8.0,
     'lambda_k2': 64.0,
     'subln_g': 7.78,
     'rel_bias': 3.884}
    for name, (base, spread) in spreads.items():
        noise = np.random.default_rng([zlib.crc32(name.encode()), seed]).standard_normal(out[name].shape)
        drawn = base * np.exp(spread * noise) if base else spread * noise
        out[name] = __import__('jax').numpy.asarray(drawn.astype(out[name].dtype))
    for name, factor in factors.items():
        out[name] = (out[name] * factor).astype(out[name].dtype)
    return out
```

```python
import math
from contextlib import ExitStack

import concourse.bass as bass
from concourse import mybir
from concourse.alu_op_type import AluOpType as ALU

F32 = mybir.dt.float32
F32R = mybir.dt.float32r
BF16 = mybir.dt.bfloat16
ACT = mybir.ActivationFunctionType
AX = mybir.AxisListType

P = 128
D = 1024
S = 1024
NB = S // P
KT = D // P
HD = 64
UNITS = 8
SB_UNITS = 4
EPS = 1e-6
NEG = -1e30
LAMBDA_INIT = 0.8 - 0.6 * math.exp(-0.3 * 0)
N_BUCKETS = 32
MAX_DISTANCE = 128
TV = 383

K_, Q_, V_, G_ = range(4)
GROUP_COL = {K_: 512, Q_: 0, V_: 1024, G_: 1536}
SB_COL = 2048

ORDER = [7, 6, 5, 4, 3, 2, 1, 0]
STEPS = [(i, m) for i in ORDER for m in range(2)]
HEAD_PIECES = 6
SLOTS = 19
PIECES = 24


def pieces_of_slot(t):
    rest = PIECES - HEAD_PIECES
    lo, hi = rest * t // SLOTS, rest * (t + 1) // SLOTS
    return range(HEAD_PIECES + lo, HEAD_PIECES + hi)


def split_points(w1=True, w2=True):
    done = {p: t for t in range(SLOTS) for p in pieces_of_slot(t)}
    pts = {}
    if w1:
        pts.setdefault(-1, []).append(1)
        pts.setdefault(0, []).append(2)
        pts.setdefault(done[11] + 1, []).append(3)
    if w2:
        pts.setdefault(done[17] + 1, []).append(4)
    return pts


def groups_ending(pieces):
    return [(p // 6, (p % 6) // 3) for p in pieces if p % 3 == 2]


def buckets_by_distance():
    exact = N_BUCKETS // 2
    out = []
    for n in range(256):
        b = n if n < exact else min(
            N_BUCKETS - 1, exact + int(math.log(n / exact) / math.log(MAX_DISTANCE / exact) * (N_BUCKETS - exact)))
        if b < len(out):
            out[b][1] = n
        else:
            while len(out) < b:
                out.append(None)
            out.append([n, n])
    return out


def n(count):
    return count + 1


def sb_tgroups_before(step):
    return 2 + sum((STEPS[s][0] + 4) // 4 for s in range(step))


def da_tgroups_before(b):
    return 2 + sum((ORDER[j] + 4) // 4 for j in range(b))


SB_TG = sb_tgroups_before(16)
DA_TG = da_tgroups_before(8)


class Unit:

    def __init__(self, U, sb):
        self.U, self.sb = U, sb
        self.qk = 16 * U
        self.mixed = 8 * U
        self.w = 16 * U if sb else 8 * U + 32
        self.tg = SB_TG * U if sb else DA_TG * U + (SB_UNITS * (SB_TG - DA_TG))
        self.da = None if sb else U - SB_UNITS

    def transposed(self, steps):
        return self.tg + (sb_tgroups_before(steps) if self.sb else da_tgroups_before(steps))


def layer_kernel(nc, x, c, norm_g, w_ada, b_ada, w_in, lq1, lk1, lq2, lk2, subln_g, w_out, rel_bias, final_g, out):
    ctx = ExitStack()
    with ctx:
        def sb(name, shape, dt=F32):
            return ctx.enter_context(nc.sbuf_tensor(name, shape, dt))

        def psum(name, shape):
            return ctx.enter_context(nc.psum_tensor(name, shape, F32))

        def sem(name):
            return ctx.enter_context(nc.semaphore(name))

        h_hi = sb("h_hi", [P, KT, S], F32R)
        h_lo = sb("h_lo", [P, KT, S], F32R)
        mixed = sb("mixed", [P, KT * S])
        st = sb("st", [P, 4, S])
        qs = sb("qs", [P, 2, S], F32R)
        kh = sb("kh", [P, 2, S], F32R)
        kl = sb("kl", [P, 2, S], F32R)
        vv = sb("vv", [P, NB, P])
        sg = sb("sg", [P, S])
        w_raw = sb("w_raw", [P, 2, KT, P])
        w_hi = sb("w_hi", [P, 2, KT, P], F32R)
        w_lo = sb("w_lo", [P, 2, KT, P], F32R)
        work = sb("work", [P, 8256])
        prob = [work[:, j * 1024:(j + 1) * 1024] for j in range(3)]
        beta = [work[:, (3 + j) * 1024:(4 + j) * 1024] for j in range(2)]
        wT = [work[:, (5 + j) * 1024:(6 + j) * 1024] for j in range(2)]
        stick = work[:, 7 * 1024:7 * 1024 + 1032]
        o_sb = sb("o_sb", [P, P])
        sq_sb = sb("sq_sb", [P, P])
        bias_hi = sb("bias_hi", [P, 256], F32R)
        bias_lo = sb("bias_lo", [P, 256], F32R)
        ident = sb("ident", [P, P])
        ident_r = sb("ident_r", [P, P], F32R)
        ident_bf = sb("ident_bf", [P, P], BF16)
        mask_bf = sb("mask_bf", [P, P], BF16)
        cols = sb("cols", [P, 96])
        c_col, sc_col = cols[:, 0:8], cols[:, 8:16]
        g_col, a_col = cols[:, 16:24], cols[:, 24:32]
        b_col = cols[:, 32:48]
        mod_col = cols[:, 48:64]
        sub_col, gs_col = cols[:, 64:65], cols[:, 65:66]
        nlam, lam_dot, lam_exp = cols[:, 66:67], cols[:, 68:70], cols[:, 70:72]
        lam_tmp = cols[:, 72:73]
        stat = sb("stat", [P, 96])
        neg_max, row_sum, inv_sum = stat[:, 0:16], stat[:, 16:32], stat[:, 32:48]
        ratio, ms, rstd, half = stat[:, 48:56], stat[:, 56:64], stat[:, 64:72], stat[:, 72:73]
        sum_sq = stat[:, 80:88]
        rb = sb("rb", [4, N_BUCKETS])
        rv = sb("rv", [4, 384])
        ones_row = vv[:, 0, :]
        toeplitz = nc.dram_tensor("toeplitz", (4, 384), F32, kind="Internal")

        z = [psum(f"z{j}", [P, 1024]) for j in range(2)]
        tp = [psum(f"tp{j}", [P, 4, P]) for j in range(2)]
        oo = psum("oo", [P, 512])
        pp = psum("pp", [P, 512])

        consts, ident_ok, ld_small, ld_lam, sc_ok, lam_ok = map(
            sem, ("consts", "ident_ok", "ld_small", "ld_lam", "sc_ok", "lam_ok"))
        ld_ada = [sem(f"ld_ada{j}") for j in range(4)]
        ld_x = [sem(f"ld_x{j}") for j in range(4)]
        sig_c, ada_used, mod_ok, rv_ok, st_rv, dve_pro = map(
            sem, ("sig_c", "ada_used", "mod_ok", "rv_ok", "st_rv", "dve_pro"))
        x_sq, x_ms, x_rs, x_scaled, xt_done, xt_free, h_hi_ok, h_ok = map(
            sem, ("x_sq", "x_ms", "x_rs", "x_scaled", "xt_done", "xt_free", "h_hi_ok", "h_ok"))
        ld_w = [sem(f"ld_w{j}") for j in range(2)]
        whi_ok, wlo_ok, p_done, p_free = map(sem, ("whi_ok", "wlo_ok", "p_done", "p_free"))
        kh_ok, qh_ok, kl_ok, ql_ok, dup_ok, sg_sig, sg_ok = map(
            sem, ("kh_ok", "qh_ok", "kl_ok", "ql_ok", "dup_ok", "sg_sig", "sg_ok"))
        qk_done, z_free, keep_ok, scan_ok, w_ok, sq_ok, tg_done, tg_free, pv_done = map(
            sem, ("qk_done", "z_free", "keep_ok", "scan_ok", "w_ok", "sq_ok", "tg_done", "tg_free", "pv_done"))
        o_ok, ot_done, mixed_ok, max_ok, bias_hi_ok, bias_ok, ld_bias = map(
            sem, ("o_ok", "ot_done", "mixed_ok", "max_ok", "bias_hi_ok", "bias_ok", "ld_bias"))
        inv_ok, ratio_ok, onorm_ok, ssq_ok, ms_ok, rstd_ok = map(
            sem, ("inv_ok", "ratio_ok", "onorm_ok", "ssq_ok", "ms_ok", "rstd_ok"))
        ld_gate = [sem(f"ld_gate{j}") for j in range(4)]
        ld_bg, ld_fg, cb_ok, gate_used, gate_ok = map(sem, ("ld_bg", "ld_fg", "cb_ok", "gate_used", "gate_ok"))
        ld_xr = [sem(f"ld_xr{j}") for j in range(2)]
        mh_ok, ml_ok, y_done, yg_ok, r_ok, f_sq, f_ms, f_rs, f_ok = map(
            sem, ("mh_ok", "ml_ok", "y_done", "yg_ok", "r_ok", "f_sq", "f_ms", "f_rs", "f_ok"))
        st_out = [sem(f"st_out{j}") for j in range(2)]

        block = ctx.enter_context(nc.Block())

        def gate_tile(j):
            return st[:, j % 4 // 2, (j % 2) * 512:(j % 2 + 1) * 512]

        def w_tile_src(col):
            return w_in[0, :, bass.ds(col, P)].rearrange("(k p) n -> p k n", p=P)

        def x_evac(act, b):
            for gidx in range(2):
                act.wait_ge(xt_done, 2 * b + gidx + 1)
                nc.scalar.activation(
                    mixed[:].rearrange("p (k s) -> p k s", k=KT)[:, 4 * gidx:4 * gidx + 4, b * P:(b + 1) * P],
                    tp[gidx][:], ACT.Copy).then_inc(xt_free, 1)

        @block.sync
        def _(sp):
            def load_w(U, t, base):
                sp.dma_start(w_raw[:, t % 2], w_tile_src(base + GROUP_COL[t] + P * U)).then_inc(ld_w[t % 2], 16)

            def dup(U):
                for src, ok in ((kh, kh_ok), (kl, kl_ok)):
                    sp.wait_ge(ok, 2 * U + 2)
                    sp.dma_start(src[HD:P, 0, :].bitcast(F32), src[0:HD, 0, :].bitcast(F32)).then_inc(dup_ok, 16)
                    sp.dma_start(src[0:HD, 1, :].bitcast(F32), src[HD:P, 1, :].bitcast(F32)).then_inc(dup_ok, 16)

            def body(U, base1, base2, w1=True, w2=True):
                dup(U)
                if w1:
                    sp.wait_ge(wlo_ok, 4 * U + 6)
                    load_w(U + 1, 3, base1)
                if w2:
                    for t in range(3):
                        sp.wait_ge(wlo_ok, 4 * U + 7 + t)
                        load_w(U + 2, t, base2)

            def load_x(b):
                if b >= 4:
                    sp.wait_ge(xt_done, 2 * (b - 4) + 2)
                sp.dma_start(st[:, b % 4, :], x[0, b * P:(b + 1) * P, :]).then_inc(ld_x[b % 4], 16)

            def load_ada(k):
                if k >= 4:
                    sp.wait_ge(ada_used, k - 3)
                sp.dma_start(work[:, (k % 4) * 2048:(k % 4 + 1) * 2048],
                             w_ada[0, k * P:(k + 1) * P, 0:2048]).then_inc(ld_ada[k % 4], 16)

            for k in range(4):
                load_ada(k)
                load_x(k)
            for k in range(4, 8):
                load_ada(k)
                load_x(k)
            for t in range(2):
                load_w(0, t, SB_COL)
            sp.wait_ge(rv_ok, 1)
            sp.dma_start(toeplitz.ap()[:, 0:TV], rv[:, 0:TV]).then_inc(st_rv, 16)
            for j in range(2, 7):
                sp.wait_ge(wlo_ok, j - 1)
                load_w(j // 4, j % 4, SB_COL)

            with sp.Fori(0, SB_UNITS - 2) as U:
                body(U, SB_COL, SB_COL)
            body(2, SB_COL, -512)
            body(3, -512, -512)
            sp.wait_ge(w_ok, n(16 * SB_UNITS))
            sp.wait_ge(st_rv, 16)
            for h in range(4):
                sp.dma_start(stick[:, h * 256:(h + 1) * 256],
                             bass.AP(toeplitz, h * 384, [[1, P], [1, 256]])).then_inc(ld_bias, 16)
            with sp.Fori(4, 6) as U:
                body(U, -512, -512)
            body(6, -512, -512, w2=False)
            dup(7)

            for k in range(KT):
                sp.wait_ge(wlo_ok, 31 + k)
                sp.dma_start(w_raw[:, k % 2].rearrange("p k n -> p (k n)"),
                             w_out[0, k * P:(k + 1) * P, :]).then_inc(ld_w[k % 2], 16)
                for j in (2 * k, 2 * k + 1):
                    if j >= 4:
                        sp.wait_ge(gate_used, j - 3)
                    else:
                        sp.wait_ge(ql_ok, 16)
                    sp.dma_start(gate_tile(j), w_ada[0, (j % 8) * P:(j % 8 + 1) * P,
                                                     2 * D + j // 8 * 512:2 * D + (j // 8 + 1) * 512]
                                 ).then_inc(ld_gate[j % 4], 16)
                if k == 2:
                    sp.wait_ge(sg_ok, 8)
                    sp.dma_start(st[:, G_, :], b_ada[:, 2 * D:3 * D].to_broadcast([P, D])).then_inc(ld_bg, 16)
            sp.wait_ge(bias_ok, 4)
            sp.dma_start(stick[:, 0:D], final_g.rearrange("(a n) -> a n", a=1).to_broadcast([P, D])).then_inc(ld_fg, 16)
            sp.wait_ge(w_ok, n(96))
            sp.wait_ge(tg_done, n(Unit(UNITS, False).tg))
            for b in range(2):
                sp.dma_start(prob[b], x[0, b * P:(b + 1) * P, :]).then_inc(ld_xr[b], 16)
            for b in range(NB):
                sp.wait_ge(f_ok, b + 1)
                sp.dma_start(out[0, b * P:(b + 1) * P, :], wT[b % 2]).then_inc(st_out[b % 2], 16)
                if b + 2 < NB:
                    sp.wait_ge(r_ok, b + 1)
                    sp.dma_start(prob[b % 2], x[0, (b + 2) * P:(b + 3) * P, :]).then_inc(ld_xr[b % 2], 16)
            for j in range(2):
                sp.wait_ge(st_out[j], 16 * NB // 2)

        @block.gpsimd
        def _(pool):
            g = nc.gpsimd
            g.memset(ident[:], 0.0).then_inc(consts, 1)
            g.memset(mask_bf[:], 0.0).then_inc(consts, 1)
            g.memset(half, -0.5).then_inc(consts, 1)
            pool.wait_ge(consts, 3)
            g.affine_select(out=ident[:], in_=ident[:], compare_op=ALU.not_equal, fill=1.0, base=0,
                            pattern=[[-1, P]], channel_multiplier=1).then_inc(ident_ok, 1)
            g.affine_select(out=mask_bf[:], in_=mask_bf[:], compare_op=ALU.is_gt, fill=NEG, base=0,
                            pattern=[[-1, P]], channel_multiplier=1).then_inc(ident_ok, 1)

            def split_lo(j, t):
                pool.wait_ge(whi_ok, j + 1)
                g.tensor_tensor(w_lo[:, t % 2], w_raw[:, t % 2], w_hi[:, t % 2], ALU.subtract).then_inc(wlo_ok, 1)

            for b in range(NB):
                pool.wait_ge(x_ms, b + 1)
                g.tensor_tensor(rstd[:, b:b + 1], ms[:, b:b + 1], half, ALU.pow).then_inc(x_rs, 1)
            for t in range(5):
                split_lo(t, t % 4)

            def body(U, sbk, w1=True, w2=True):
                un = Unit(U, sbk)
                ready = split_points(w1, w2)
                for t in [-1] + list(range(SLOTS)):
                    if not sbk and t >= 4 and t % 2 == 0:
                        b = (t - 4) // 2
                        pool.wait_ge(ms_ok, 8 * un.da + b + 1)
                        g.tensor_tensor(rstd[:, b:b + 1], ms[:, b:b + 1], half, ALU.pow).then_inc(rstd_ok, 1)
                    for j in ready.get(t, ()):
                        split_lo(4 * U + 4 + j, j % 4)
                    if not w1 and t % 2 and 0 < t < 16:
                        out_lo(t // 2)

            def out_lo(k):
                pool.wait_ge(whi_ok, 33 + k)
                g.tensor_tensor(h_lo[:, k, :], w_raw[:, k % 2].rearrange("p k n -> p (k n)"),
                                h_hi[:, k, :], ALU.subtract).then_inc(wlo_ok, 1)

            with pool.Fori(0, SB_UNITS) as U:
                body(U, True)
            with pool.Fori(4, 6) as U:
                body(U, False)
            body(6, False, w2=False)
            body(7, False, False, False)
            for b in range(NB):
                pool.wait_ge(f_ms, b + 1)
                g.tensor_tensor(rstd[:, b:b + 1], ms[:, b:b + 1], half, ALU.pow).then_inc(f_rs, 1)

        @block.scalar
        def _(act):
            s = nc.scalar
            for sem_ in (p_free, z_free, tg_free):
                act.sem_inc(sem_, 1)
            with nc.allow_non_contiguous_dma(reason="small per-feature columns"):
                for dst, src in ((c_col, c.rearrange("a (k p) -> p (a k)", p=P)),
                                 (g_col, norm_g.rearrange("a (k p) -> p (a k)", p=P)),
                                 (b_col, b_ada[:, 0:2048].rearrange("a (k p) -> p (a k)", p=P)),
                                 (sub_col, subln_g.rearrange("a (k p) -> p (a k)", p=P)),
                                 (rb[:, :], rel_bias.rearrange("b h -> h b"))):
                    act.dma_start(dst, src).then_inc(ld_small, 16)
            for j, v in enumerate((lq1, lk1, lq2, lk2)):
                act.dma_start(sg[:, j * HD:(j + 1) * HD], v.to_broadcast([P, HD])).then_inc(ld_lam, 16)
            act.wait_ge(ld_small, 80)
            s.activation(sc_col, c_col, ACT.Sigmoid).then_inc(sig_c, 1)
            for b in range(NB):
                act.wait_ge(ld_x[b % 4], 16 * (b // 4 + 1))
                if b:
                    act.wait_ge(x_sq, b)
                s.activation(vv[:].rearrange("p a b -> p (a b)"), st[:, b % 4, :], ACT.Square,
                             accum_out=sum_sq[:, b:b + 1]).then_inc(x_sq, 1)
                if b:
                    x_evac(act, b - 1)
            x_evac(act, NB - 1)
            act.wait_ge(lam_ok, 2)
            s.activation(lam_exp, lam_dot, ACT.Exp).then_inc(sig_c, 1)
            act.wait_ge(mod_ok, 1)
            act.wait_ge(xt_free, 2 * NB)
            for k in range(KT):
                s.activation(h_hi[:, k, :], mixed[:, k * S:(k + 1) * S], ACT.Identity,
                             bias=mod_col[:, k:k + 1], scale=a_col[:, k:k + 1]).then_inc(h_hi_ok, 1)

            def p_evac(U1, t, c_, st_free):
                act.wait_ge(p_done, n(8 * U1 + 2 * t + c_ + 1))
                for sem_, v in st_free:
                    act.wait_ge(sem_, v)
                s.activation(st[:, t, c_ * 512:(c_ + 1) * 512], pp[:], ACT.Copy,
                             scale=HD ** -0.5 if t == Q_ else 1.0).then_inc(p_free, 1)

            for t in range(4):
                for c_ in range(2):
                    p_evac(0, t, c_, ((xt_done, 2 * NB),))

            def t_evac(un, index, dst, j0, cnt, wait=()):
                act.wait_ge(tg_done, n(un.tg + index + 1))
                for sem_, v in wait:
                    act.wait_ge(sem_, v)
                s.activation(dst[:, j0 * P:(j0 + cnt) * P], tp[index % 2][:, 0:cnt, :].rearrange("p a b -> p (a b)"),
                             ACT.Copy).then_inc(tg_free, 1)

            def body(U, sbk, w1=True):
                un = Unit(U, sbk)
                vflat = vv[:].rearrange("p a b -> p (a b)")

                def evac_next(t, c_):
                    free = {K_: ((kl_ok, 2 * U + 2),), Q_: ((ql_ok, 2 * U + 2),),
                            V_: ((tg_done, n(un.tg + 2)),), G_: ((sg_ok, U + 1),)}[t]
                    p_evac(U + 1, t, c_, free)

                act.wait_ge(qk_done, n(un.qk))
                act.wait_ge(p_free, n(8 * U + 8))
                s.activation(kh[0:HD, 0, :], st[0:HD, K_, :], ACT.Copy).then_inc(kh_ok, 1)
                s.activation(kh[HD:P, 1, :], st[HD:P, K_, :], ACT.Copy).then_inc(kh_ok, 1)
                s.activation(qs[0:HD, 0, :], st[0:HD, Q_, :], ACT.Copy).then_inc(qh_ok, 1)
                s.activation(qs[HD:P, 1, :], st[HD:P, Q_, :], ACT.Copy).then_inc(qh_ok, 1)
                t_evac(un, 0, vflat, 0, 4, ((pv_done, n(un.w)),))
                t_evac(un, 1, vflat, 4, 4)
                if w1:
                    evac_next(0, 0)
                act.wait_ge(mixed_ok, n(un.mixed))
                s.activation(sg[:], st[:, G_, :], ACT.Sigmoid).then_inc(sg_sig, 1)
                if w1:
                    evac_next(0, 1)
                for t in range(SLOTS):
                    if t < 16:
                        i, m = STEPS[t]
                        L = (i + 1) * P
                        if sbk:
                            act.wait_ge(qk_done, n(un.qk + t + 1))
                            act.wait_ge(tg_done, n(un.transposed(t - 2) if t >= 3 else un.tg))
                            s.activation(prob[t % 3][:, 0:L], z[t % 2][:, 0:L], ACT.Sigmoid,
                                         scale=-1.0).then_inc(keep_ok, 1)
                            act.wait_ge(w_ok, n(un.w + (t - 1 if t >= 2 else 0)))
                            s.activation(beta[t % 2][:, 0:L], z[t % 2][:, 0:L], ACT.Sigmoid).then_inc(z_free, 1)
                        else:
                            b = t // 2
                            act.wait_ge(max_ok, 16 * un.da + t + 1)
                            if m == 0:
                                act.wait_ge(tg_done, n(un.transposed(b - 1) if b >= 2 else un.tg))
                            else:
                                act.wait_ge(w_ok, n(un.w + (b - 1 if b >= 2 else 0)))
                            dst = prob[b % 2] if m == 0 else beta[b % 2]
                            s.activation(dst[:, 0:L], z[t % 2][:, 0:L], ACT.Exp, bias=neg_max[:, t:t + 1],
                                         accum_out=row_sum[:, t:t + 1]).then_inc(z_free, 1)
                    if sbk and 2 <= t < 18:
                        evac_step(un, t - 2, STEPS[t - 2][0], sb_tgroups_before(t - 2))
                    if not sbk and t >= 3 and t % 2 and t < 18:
                        b = (t - 3) // 2
                        evac_step(un, b, ORDER[b], da_tgroups_before(b))
                    if w1:
                        for tt, cc in groups_ending(pieces_of_slot(t)):
                            evac_next(tt, cc)

            def evac_step(un, k, i, g0):
                wait = ((pv_done, n(un.w + (k - 1 if k >= 2 else 0))),)
                for gidx, j0 in enumerate(range(0, i + 1, 4)):
                    t_evac(un, g0 + gidx, wT[k % 2], j0, min(4, i + 1 - j0), wait)

            with act.Fori(0, SB_UNITS) as U:
                body(U, True)
            with act.Fori(4, 7) as U:
                body(U, False)
            body(7, False, False)

            for b in range(NB):
                act.wait_ge(r_ok, b + 1)
                if b:
                    act.wait_ge(f_sq, b)
                s.activation(prob[2], beta[b % 2], ACT.Square, accum_out=sum_sq[:, b:b + 1]).then_inc(f_sq, 1)

        @block.vector
        def _(dve):
            v = nc.vector
            for sem_ in (mixed_ok, w_ok):
                dve.sem_inc(sem_, 1)
            chain = [0]

            def link(ins):
                chain[0] += 1
                ins.then_inc(dve_pro, 1)
                dve.wait_ge(dve_pro, chain[0])

            dve.wait_ge(ld_small, 80)
            link(v.tensor_scalar(rb[:, :], rb[:, :], rb[:, N_BUCKETS - 1:N_BUCKETS], None, ALU.subtract))
            link(v.memset(rv[:, 0:P - 1], NEG))
            for bkt, (lo, hi) in enumerate(buckets_by_distance()):
                fill = v.tensor_copy(rv[:, P - 1 + lo:P + hi], rb[:, bkt:bkt + 1].to_broadcast([4, hi - lo + 1]))
                if bkt < N_BUCKETS - 1:
                    link(fill)
            fill.then_inc(rv_ok, 1)
            dve.wait_ge(ident_ok, 1)
            v.tensor_copy(ident_r[:], ident[:]).then_inc(sc_ok, 1)
            v.tensor_copy(ident_bf[:], ident[:]).then_inc(sc_ok, 1)
            dve.wait_ge(sig_c, 1)
            v.tensor_tensor(sc_col, sc_col, c_col, ALU.mult).then_inc(sc_ok, 1)
            v.tensor_scalar(gs_col, sub_col, 1.0 - LAMBDA_INIT, None, ALU.mult).then_inc(sc_ok, 1)
            dve.wait_ge(ld_lam, 64)
            for j in range(2):
                v.tensor_tensor(sg[:, 256 + j * HD:256 + (j + 1) * HD], sg[:, 2 * j * HD:(2 * j + 1) * HD],
                                sg[:, (2 * j + 1) * HD:(2 * j + 2) * HD], ALU.mult).then_inc(dve_pro, 1)
            chain[0] += 2
            dve.wait_ge(dve_pro, chain[0])
            v.tensor_reduce(lam_dot, sg[:, 256:256 + 2 * HD].rearrange("p (a b) -> p a b", a=2), AX.X,
                            ALU.add).then_inc(lam_ok, 2)
            for b in range(NB):
                dve.wait_ge(x_sq, b + 1)
                v.tensor_scalar(ms[:, b:b + 1], sum_sq[:, b:b + 1], 1.0 / D, EPS, ALU.mult, ALU.add).then_inc(x_ms, 1)
                dve.wait_ge(x_rs, b + 1)
                v.tensor_scalar(st[:, b % 4, :], st[:, b % 4, :], rstd[:, b:b + 1], None, ALU.mult).then_inc(x_scaled, 1)
            dve.wait_ge(sig_c, 2)
            link(v.tensor_scalar(lam_tmp, lam_exp[:, 1:2], -LAMBDA_INIT, None, ALU.add))
            link(v.tensor_tensor(nlam, lam_tmp, lam_exp[:, 0:1], ALU.subtract))
            dve.wait_ge(ada_used, 8)
            link(v.tensor_tensor(mod_col, z[0][:, 0:16], b_col, ALU.add))
            v.scalar_tensor_tensor(a_col, mod_col[:, 8:16], 1.0, g_col, ALU.add, ALU.mult).then_inc(mod_ok, 1)
            dve.wait_ge(mod_ok, 1)

            def split_hi(U1, t, first=False):
                dve.wait_ge(ld_w[t % 2], 32 * U1 + 16 * (t // 2 + 1))
                if not first:
                    dve.wait_ge(p_done, n(8 * U1 + 2 * t - 2))
                v.tensor_copy(w_hi[:, t % 2], w_raw[:, t % 2]).then_inc(whi_ok, 1)

            for t in range(2):
                split_hi(0, t, True)
            for k in range(KT):
                xk = mixed[:, k * S:(k + 1) * S]
                dve.wait_ge(h_hi_ok, k + 1)
                link(v.tensor_scalar(xk, xk, a_col[:, k:k + 1], mod_col[:, k:k + 1], ALU.mult, ALU.add))
                v.tensor_tensor(h_lo[:, k, :], xk, h_hi[:, k, :], ALU.subtract).then_inc(h_ok, 1)
            for t in range(2, 5):
                split_hi(t // 4, t % 4)
            v.memset(stick[:, :], 1.0).then_inc(dve_pro, 1)
            chain[0] += 1
            dve.wait_ge(dve_pro, chain[0])

            def commit(U, un):
                dve.wait_ge(kh_ok, 2 * U + 2)
                v.tensor_tensor(kl[0:HD, 0, :], st[0:HD, K_, :], kh[0:HD, 0, :], ALU.subtract).then_inc(kl_ok, 1)
                v.tensor_tensor(kl[HD:P, 1, :], st[HD:P, K_, :], kh[HD:P, 1, :], ALU.subtract).then_inc(kl_ok, 1)
                dve.wait_ge(qh_ok, 2 * U + 2)
                v.tensor_tensor(qs[HD:P, 0, :], st[0:HD, Q_, :], qs[0:HD, 0, :], ALU.subtract).then_inc(ql_ok, 1)
                v.tensor_tensor(qs[0:HD, 1, :], st[HD:P, Q_, :], qs[HD:P, 1, :], ALU.subtract).then_inc(ql_ok, 1)

            def body(U, sbk, w1=True, w2=True):
                un = Unit(U, sbk)
                ready = split_points(w1, w2)

                def splits(t):
                    for j in ready.get(t, ()):
                        split_hi(U + 1 + j // 4, j % 4)
                    if not w1:
                        last_unit_work(t)

                commit(U, un)
                if not sbk:
                    dve.wait_ge(ld_bias, 64)
                    braw = stick[:, bass.ds(un.da * 256, 256)]
                    v.tensor_copy(bias_hi[:, ::-1], braw).then_inc(bias_hi_ok, 1)
                    dve.wait_ge(bias_hi_ok, un.da + 1)
                    v.tensor_tensor(bias_lo[:, ::-1], braw, bias_hi[:, ::-1], ALU.subtract).then_inc(bias_ok, 1)
                splits(-1)
                for t in range(SLOTS):
                    b = (t - 4) // 2 if t >= 4 and t % 2 == 0 else None
                    if sbk:
                        if b is not None:
                            dve.wait_ge(pv_done, n(un.w + 2 * b + 2))
                            dve.wait_ge(ot_done, n(un.mixed + b))
                            v.tensor_copy(o_sb[:], oo[:, 0:P]).then_inc(o_ok, 1)
                        if t < 16:
                            L = (STEPS[t][0] + 1) * P
                            dve.wait_ge(keep_ok, un.qk + t + 1)
                            dve.wait_ge(w_ok, n(un.w + t))
                            kp = prob[t % 3][:, 0:L][:, ::-1]
                            v.tensor_tensor_scan(stick[:, 0:L][:, ::-1], kp, kp, 1.0,
                                                 ALU.mult, ALU.bypass).then_inc(scan_ok, 1)
                    else:
                        if b is not None:
                            da_leave_1(un, b)
                        if t < 16:
                            L = (STEPS[t][0] + 1) * P
                            dve.wait_ge(qk_done, n(un.qk + t + 1))
                            v.tensor_reduce(neg_max[:, t:t + 1], z[t % 2][:, 0:L], AX.X, ALU.max,
                                            negate=True).then_inc(max_ok, 1)
                        if b is not None:
                            da_leave_2(un, b)
                        if t >= 2 and t % 2 == 0 and t <= 16:
                            combine(un, t // 2 - 1)
                    if t == 3:
                        dve.wait_ge(sg_sig, U + 1)
                        v.tensor_tensor(sg[:], sg[:], st[:, G_, :], ALU.mult).then_inc(sg_ok, 1)
                    if b is not None:
                        i = ORDER[b]
                        dve.wait_ge(ot_done, n(un.mixed + b + 1))
                        dve.wait_ge(sg_ok, U + 1)
                        gate = sg[:, i * P:(i + 1) * P]
                        if sbk:
                            v.tensor_tensor(mixed[:, bass.ds((U + 4) * S + i * P, P)], oo[:, P:2 * P], gate,
                                            ALU.mult).then_inc(mixed_ok, 1)
                        else:
                            v.scalar_tensor_tensor(mixed[:, bass.ds((U - 4) * S + i * P, P)], oo[:, P:2 * P],
                                                   gs_col, gate, ALU.mult, ALU.mult).then_inc(mixed_ok, 1)
                    if sbk and t < 16:
                        dve.wait_ge(z_free, n(un.qk + t + 1))
                        dve.wait_ge(scan_ok, un.qk + t + 1)
                        v.tensor_tensor(prob[t % 3][:, 0:L], beta[t % 2][:, 0:L], stick[:, 1:L + 1],
                                        ALU.mult).then_inc(w_ok, 1)
                    splits(t)

            def last_unit_work(t):
                if t == -1:
                    dve.wait_ge(tg_done, n(Unit(7, False).tg + 2))
                    for j in range(KT):
                        v.tensor_scalar(st[:, V_, j * P:(j + 1) * P], ident[:], 0.0, sc_col[:, j:j + 1],
                                        ALU.mult, ALU.add).then_inc(cb_ok, 1)
                if t % 2 and 0 < t < 16:
                    k = t // 2
                    dve.wait_ge(ld_w[k % 2], 16 * (16 + k // 2 + 1))
                    v.tensor_copy(h_hi[:, k, :], w_raw[:, k % 2].rearrange("p k n -> p (k n)")).then_inc(whi_ok, 1)
                if t in (8, 16):
                    half_ = slice((t // 16) * 512, (t // 16 + 1) * 512)
                    dve.wait_ge(gate_used, t)
                    dve.wait_ge(ld_bg, 16)
                    v.tensor_tensor(st[:, G_, half_], pp[:], st[:, G_, half_], ALU.add).then_inc(gate_ok, 1)

            def combine(un, b):
                i = ORDER[b]
                L = (i + 1) * P
                t0 = 2 * b
                dve.wait_ge(z_free, n(un.qk + t0 + 2))
                v.reciprocal(inv_sum[:, t0:t0 + 2], row_sum[:, t0:t0 + 2]).then_inc(inv_ok, 1)
                dve.wait_ge(inv_ok, 8 * un.da + b + 1)
                v.tensor_scalar(ratio[:, b:b + 1], row_sum[:, t0:t0 + 1], inv_sum[:, t0 + 1:t0 + 2], nlam,
                                ALU.mult, ALU.mult).then_inc(ratio_ok, 1)
                dve.wait_ge(ratio_ok, 8 * un.da + b + 1)
                v.scalar_tensor_tensor(prob[b % 2][:, 0:L], beta[b % 2][:, 0:L], ratio[:, b:b + 1],
                                       prob[b % 2][:, 0:L], ALU.mult, ALU.add).then_inc(w_ok, 1)

            def da_leave_1(un, b):
                dve.wait_ge(pv_done, n(un.w + b + 1))
                dve.wait_ge(ot_done, n(un.mixed + b))
                v.tensor_scalar(o_sb[:], oo[:, 0:P], inv_sum[:, 2 * b:2 * b + 1], None, ALU.mult).then_inc(onorm_ok, 1)
                dve.wait_ge(onorm_ok, 8 * un.da + b + 1)
                v.tensor_tensor(sq_sb[:], o_sb[:], o_sb[:], ALU.mult).then_inc(sq_ok, 1)
                dve.wait_ge(sq_ok, 8 * un.da + b + 1)
                v.tensor_reduce(sum_sq[:, b:b + 1], sq_sb[:], AX.X, ALU.add).then_inc(ssq_ok, 1)
                dve.wait_ge(ssq_ok, 8 * un.da + b + 1)
                v.tensor_scalar(ms[:, b:b + 1], sum_sq[:, b:b + 1], 1.0 / P, EPS, ALU.mult, ALU.add).then_inc(ms_ok, 1)

            def da_leave_2(un, b):
                dve.wait_ge(rstd_ok, 8 * un.da + b + 1)
                v.tensor_scalar(o_sb[:], o_sb[:], rstd[:, b:b + 1], None, ALU.mult).then_inc(o_ok, 1)

            with dve.Fori(0, SB_UNITS) as U:
                body(U, True)
            with dve.Fori(4, 6) as U:
                body(U, False)
            body(6, False, w2=False)
            body(7, False, False, False)

            mT = mixed[:].rearrange("p (k s) -> p k s", k=KT)

            def split_mixed(b):
                if b >= 2:
                    dve.wait_ge(y_done, b - 1)
                v.tensor_copy(w_hi[:, b % 2], mT[:, :, b * P:(b + 1) * P]).then_inc(mh_ok, 1)
                dve.wait_ge(mh_ok, b + 1)
                v.tensor_tensor(w_lo[:, b % 2], mT[:, :, b * P:(b + 1) * P], w_hi[:, b % 2],
                                ALU.subtract).then_inc(ml_ok, 1)

            def final_scale(b):
                dve.wait_ge(f_sq, b + 1)
                v.tensor_scalar(ms[:, b:b + 1], sum_sq[:, b:b + 1], 1.0 / D, EPS, ALU.mult, ALU.add).then_inc(f_ms, 1)
                dve.wait_ge(f_rs, b + 1)
                if b >= 2:
                    dve.wait_ge(st_out[b % 2], 16 * (b // 2))
                v.scalar_tensor_tensor(wT[b % 2], beta[b % 2], rstd[:, b:b + 1], stick[:, 0:D],
                                       ALU.mult, ALU.mult).then_inc(f_ok, 1)

            dve.wait_ge(mixed_ok, n(64))
            dve.wait_ge(p_done, n(64))
            split_mixed(0)
            dve.wait_ge(ld_fg, 16)
            for b in range(NB):
                if b + 1 < NB:
                    split_mixed(b + 1)
                dve.wait_ge(y_done, b + 1)
                if b >= 2:
                    dve.wait_ge(f_ok, b - 1)
                v.tensor_tensor(beta[b % 2], z[b % 2][:, :], st[:, G_, :], ALU.mult).then_inc(yg_ok, 1)
                dve.wait_ge(yg_ok, b + 1)
                dve.wait_ge(ld_xr[b % 2], 16 * (b // 2 + 1))
                v.tensor_tensor(beta[b % 2], beta[b % 2], prob[b % 2], ALU.add).then_inc(r_ok, 1)
                if b:
                    final_scale(b - 1)
            final_scale(NB - 1)

        @block.tensor
        def _(pe):
            t_ = nc.tensor
            for sem_ in (p_done, qk_done, tg_done, pv_done, ot_done):
                pe.sem_inc(sem_, 1)

            def transpose_x(b):
                pe.wait_ge(x_scaled, b + 1)
                for gidx in range(2):
                    if b:
                        pe.wait_ge(xt_free, 2 * b + gidx - 1)
                    for j in range(4):
                        k = 4 * gidx + j
                        tr = t_.transpose(tp[gidx][:, j, :], st[:, b % 4, k * P:(k + 1) * P], ident[:])
                    tr.then_inc(xt_done, 1)

            pe.wait_ge(ident_ok, 2)
            pe.wait_ge(sc_ok, 4)
            for k in range(KT):
                pe.wait_ge(ld_ada[k % 4], 16 * (k // 4 + 1))
                for j in range(16):
                    mm = t_.matmul(z[0][:, j:j + 1], work[:, (k % 4) * 2048 + j * P:(k % 4) * 2048 + (j + 1) * P],
                                   sc_col[:, k:k + 1], start=(k == 0 and j == 0), stop=(k == KT - 1),
                                   skip_group_check=True)
                mm.then_inc(ada_used, 1)
                transpose_x(k)

            def piece(U1, p, first=False):
                t, c_, pas = p // 6, p % 6 // 3, p % 3
                if p % 6 == 0:
                    pe.wait_ge(wlo_ok, 4 * U1 + t + 1)
                if pas == 0:
                    if not (first and p == 0):
                        pe.wait_ge(p_free, n(8 * U1 + 2 * t + c_))
                lhs = w_lo if pas == 2 else w_hi
                rhs = h_lo if pas == 1 else h_hi
                for k in range(KT):
                    if first and p == 0:
                        pe.wait_ge(h_ok, k + 1)
                    mm = t_.matmul(pp[:], lhs[:, t % 2, k, :], rhs[:, k, c_ * 512:(c_ + 1) * 512],
                                   start=(pas == 0 and k == 0), stop=(pas == 2 and k == KT - 1))
                if pas == 2:
                    mm.then_inc(p_done, 1)

            for p in range(PIECES):
                piece(0, p, True)

            def logits(un, t):
                i, m = STEPS[t]
                L = (i + 1) * P
                pe.wait_ge(z_free, n(un.qk + (t - 1 if t >= 2 else 0)))
                for ch in range(0, L, 512):
                    e = min(ch + 512, L)
                    q = qs[:, m, i * P:(i + 1) * P]
                    if un.sb:
                        adds = [(ident_bf, mask_bf, i * P, (i + 1) * P, 0)]
                    else:
                        adds = [(ident_r, bb, lo, hi, (1 - i) * P) for bb in (bias_hi, bias_lo)
                                for lo, hi in [(max(i - 1, 0) * P, (i + 1) * P)]]
                    adds = [(a, bb, max(lo, ch), min(hi, e), off) for a, bb, lo, hi, off in adds if max(lo, ch) < min(hi, e)]
                    t_.matmul(z[t % 2][:, ch:e], q, kh[:, m, ch:e], start=True, stop=False)
                    mm = t_.matmul(z[t % 2][:, ch:e], q, kl[:, m, ch:e], start=False, stop=not adds)
                    for x_, (a, bb, lo, hi, off) in enumerate(adds):
                        if un.sb:
                            mm = t_.matmul(z[t % 2][:, lo:hi], a[:], bb[:], start=False, stop=True)
                        else:
                            mm = t_.matmul(z[t % 2][:, lo:hi], a[:], bb[:, lo + off:hi + off], start=False,
                                           stop=x_ == len(adds) - 1)
                mm.then_inc(qk_done, 1)

            def transposes(un, k, i, src, g0):
                pe.wait_ge(w_ok, n(un.w + k + 1))
                for gidx, j0 in enumerate(range(0, i + 1, 4)):
                    pe.wait_ge(tg_free, n(un.tg + g0 + gidx - 1))
                    for j in range(j0, min(j0 + 4, i + 1)):
                        tr = t_.transpose(tp[(g0 + gidx) % 2][:, j - j0, :], src[:, j * P:(j + 1) * P], ident[:])
                    tr.then_inc(tg_done, 1)

            def values(un, k, i, b, m0, m1, first):
                pe.wait_ge(tg_free, n(un.transposed(k + 1)))
                if first:
                    pe.wait_ge(mixed_ok, n(un.mixed + b))
                for j in range(i + 1):
                    mm = t_.matmul(oo[:, m0:m1], wT[k % 2][:, j * P:(j + 1) * P], vv[:, j, m0:m1],
                                   start=j == 0, stop=j == i)
                mm.then_inc(pv_done, 1)

            def body(U, sbk, w1=True):
                un = Unit(U, sbk)
                pe.wait_ge(p_free, n(8 * U + 8))
                for gidx in range(2):
                    pe.wait_ge(tg_free, n(un.tg))
                    for j in range(4):
                        tr = t_.transpose(tp[gidx][:, j, :], st[:, V_, (4 * gidx + j) * P:(4 * gidx + j + 1) * P], ident[:])
                    tr.then_inc(tg_done, 1)
                if w1:
                    for p in range(HEAD_PIECES):
                        piece(U + 1, p)
                pe.wait_ge(ql_ok, 2 * U + 2)
                pe.wait_ge(dup_ok, 64 * U + 64)
                pe.wait_ge(kl_ok, 2 * U + 2)
                if not sbk:
                    pe.wait_ge(bias_ok, un.da + 1)
                for t in range(SLOTS):
                    if t < 16:
                        logits(un, t)
                    if sbk and 2 <= t < 18:
                        transposes(un, t - 2, STEPS[t - 2][0], prob[(t - 2) % 3], sb_tgroups_before(t - 2))
                    if not sbk and t % 2 and 3 <= t < 18:
                        b = (t - 3) // 2
                        transposes(un, b, ORDER[b], prob[b % 2], da_tgroups_before(b))
                    ps = list(pieces_of_slot(t)) if w1 else []
                    for p in ps[:1]:
                        piece(U + 1, p)
                    if t >= 4 and t % 2 == 0:
                        pe.wait_ge(o_ok, un.mixed + (t - 4) // 2 + 1)
                        t_.transpose(oo[:, P:2 * P], o_sb[:], ident[:]).then_inc(ot_done, 1)
                    for p in ps[1:]:
                        piece(U + 1, p)
                    if not w1 and t < 16:
                        gate_product(t)
                    if sbk and 2 <= t < 18:
                        i, m = STEPS[t - 2]
                        values(un, t - 2, i, (t - 2) // 2, m * HD, (m + 1) * HD, m == 0)
                    if not sbk and t % 2 and 3 <= t < 18:
                        values(un, (t - 3) // 2, ORDER[(t - 3) // 2], (t - 3) // 2, 0, P, True)

            def gate_product(j):
                if j == 0:
                    pe.wait_ge(cb_ok, KT)
                if j == 8:
                    pe.wait_ge(gate_ok, 1)
                pe.wait_ge(ld_gate[j % 4], 16 * (j // 4 + 1))
                t_.matmul(pp[:], st[:, V_, (j % 8) * P:(j % 8 + 1) * P], gate_tile(j),
                          start=j % 8 == 0, stop=j % 8 == 7).then_inc(gate_used, 1)

            with pe.Fori(0, SB_UNITS) as U:
                body(U, True)
            with pe.Fori(4, 7) as U:
                body(U, False)
            body(7, False, False)

            pe.wait_ge(wlo_ok, 40)
            pe.wait_ge(z_free, n(128))
            for b in range(NB):
                pe.wait_ge(ml_ok, b + 1)
                if b >= 2:
                    pe.wait_ge(yg_ok, b - 1)
                for ch in range(2):
                    for pas in range(3):
                        lhs, rhs = (w_lo if pas == 2 else w_hi), (h_lo if pas == 1 else h_hi)
                        for k in range(KT):
                            mm = t_.matmul(z[b % 2][:, ch * 512:(ch + 1) * 512], lhs[:, b % 2, k, :],
                                           rhs[:, k, ch * 512:(ch + 1) * 512],
                                           start=(pas == 0 and k == 0), stop=(pas == 2 and k == KT - 1))
                mm.then_inc(y_done, 1)


_INS = ["x", "c", "norm_g", "w_ada", "b_ada", "w_in", "lambda_q1", "lambda_k1", "lambda_q2", "lambda_k2",
        "subln_g", "w_out", "rel_bias", "final_g"]


def kernel(**inputs):
    import numpy as _np
    import concourse.bacc as _bacc
    from concourse.bass_utils import run_bass_kernel_spmd as _run

    nc = _bacc.Bacc("TRN2", target_bir_lowering=False, num_devices=1)
    arrays, args = {}, []
    for name in _INS:
        a = _np.ascontiguousarray(inputs[name])
        arrays[f"in_{name}_dram"] = a
        args.append(nc.dram_tensor(f"in_{name}_dram", a.shape, mybir.dt.from_np(a.dtype), kind="ExternalInput").ap())
    out = nc.dram_tensor("out_0_dram", (1, S, D), F32, kind="ExternalOutput").ap()
    layer_kernel(nc, *args, out)
    r = _run(nc, [arrays], core_ids=[0])
    return r.results[0]["out_0_dram"]
```

```python
import math
from contextlib import ExitStack

import concourse.bass as bass
from concourse import mybir
from concourse.alu_op_type import AluOpType as ALU

F32 = mybir.dt.float32
F32R = mybir.dt.float32r
BF16 = mybir.dt.bfloat16
ACT = mybir.ActivationFunctionType
AX = mybir.AxisListType

P = 128
D = 1024
S = 1024
NB = S // P
KT = D // P
HD = 64
UNITS = 8
SB_UNITS = 4
EPS = 1e-6
NEG = -1e30
LAMBDA_INIT = 0.8 - 0.6 * math.exp(-0.3 * 0)
N_BUCKETS = 32
MAX_DISTANCE = 128
TV = 383

K_, Q_, V_, G_ = range(4)
GROUP_COL = {K_: 512, Q_: 0, V_: 1024, G_: 1536}
SB_COL = 2048

ORDER = [7, 6, 5, 4, 3, 2, 1, 0]
STEPS = [(i, m) for i in ORDER for m in range(2)]
HEAD_PIECES = 2
SB_SLOTS, DA_SLOTS = 20, 21
TAIL = (3, 2, 1, 0)
PIECES = 24


def pieces_of_slot(t):
    rest = PIECES - HEAD_PIECES - sum(TAIL)
    if t >= 16:
        lo = HEAD_PIECES + rest + sum(TAIL[:t - 16])
        return range(lo, lo + (TAIL[t - 16] if t - 16 < len(TAIL) else 0))
    lo, hi = rest * t // 16, rest * (t + 1) // 16
    return range(HEAD_PIECES + lo, HEAD_PIECES + hi)


def split_points(w1=True, w2=True):
    done = {p: t for t in range(SB_SLOTS) for p in pieces_of_slot(t)}
    pts = {}
    if w1:
        pts.setdefault(0, []).append(1)
        pts.setdefault(done[5] + 1, []).append(2)
        pts.setdefault(done[11] + 1, []).append(3)
    if w2:
        pts.setdefault(done[17] + 1, []).append(4)
    return pts


def groups_ending(pieces):
    return [(p // 6, (p % 6) // 3) for p in pieces if p % 3 == 2]


def buckets_by_distance():
    exact = N_BUCKETS // 2
    out = []
    for n in range(256):
        b = n if n < exact else min(
            N_BUCKETS - 1, exact + int(math.log(n / exact) / math.log(MAX_DISTANCE / exact) * (N_BUCKETS - exact)))
        if b < len(out):
            out[b][1] = n
        else:
            while len(out) < b:
                out.append(None)
            out.append([n, n])
    return out


def n(count):
    return count + 1


def sb_tgroups_before(step):
    return 2 + sum((STEPS[s][0] + 4) // 4 for s in range(step))


def da_tgroups_before(b):
    return 2 + sum((ORDER[j] + 4) // 4 for j in range(b))


SB_TG = sb_tgroups_before(16)
DA_TG = da_tgroups_before(8)


class Unit:

    def __init__(self, U, sb):
        self.U, self.sb = U, sb
        self.qk = 16 * U
        self.mixed = 8 * U
        self.w = 16 * U if sb else 8 * U + 32
        self.tg = SB_TG * U if sb else DA_TG * U + (SB_UNITS * (SB_TG - DA_TG))
        self.da = None if sb else U - SB_UNITS

    def transposed(self, steps):
        return self.tg + (sb_tgroups_before(steps) if self.sb else da_tgroups_before(steps))


def layer_kernel(nc, x, c, norm_g, w_ada, b_ada, w_in, lq1, lk1, lq2, lk2, subln_g, w_out, rel_bias, final_g, out):
    ctx = ExitStack()
    with ctx:
        def sb(name, shape, dt=F32):
            return ctx.enter_context(nc.sbuf_tensor(name, shape, dt))

        def psum(name, shape):
            return ctx.enter_context(nc.psum_tensor(name, shape, F32))

        def sem(name):
            return ctx.enter_context(nc.semaphore(name))

        h_hi = sb("h_hi", [P, KT, S], F32R)
        h_lo = sb("h_lo", [P, KT, S], F32R)
        mixed = sb("mixed", [P, KT * S])
        st = sb("st", [P, 4, S])
        qs = sb("qs", [P, 2, S], F32R)
        kh = sb("kh", [P, 2, S], F32R)
        kl = sb("kl", [P, 2, S], F32R)
        vv = sb("vv", [P, NB, P])
        sg = sb("sg", [P, S])
        w_raw = sb("w_raw", [P, 2, KT, P])
        w_hi = sb("w_hi", [P, 2, KT, P], F32R)
        w_lo = sb("w_lo", [P, 2, KT, P], F32R)
        work = sb("work", [P, 8256])
        prob = [work[:, j * 1024:(j + 1) * 1024] for j in range(3)]
        beta = [work[:, (3 + j) * 1024:(4 + j) * 1024] for j in range(2)]
        wT = [work[:, (5 + j) * 1024:(6 + j) * 1024] for j in range(2)]
        stick = work[:, 7 * 1024:7 * 1024 + 1032]
        o_sb = sb("o_sb", [P, P])
        sq_sb = sb("sq_sb", [P, P])
        bias_hi = sb("bias_hi", [P, 256], F32R)
        bias_lo = sb("bias_lo", [P, 256], F32R)
        ident = sb("ident", [P, P])
        ident_r = sb("ident_r", [P, P], F32R)
        ident_bf = sb("ident_bf", [P, P], BF16)
        mask_bf = sb("mask_bf", [P, P], BF16)
        cols = sb("cols", [P, 96])
        raw_col = cols[:, 0:33]
        c_col, g_col, b_col, sub_col = cols[:, 0:8], cols[:, 8:16], cols[:, 16:32], cols[:, 32:33]
        sc_col, a_col = cols[:, 33:41], cols[:, 41:49]
        mod_col, gs_col = cols[:, 49:65], cols[:, 65:66]
        nlam, lam_dot, lam_exp = cols[:, 66:67], cols[:, 68:70], cols[:, 70:72]
        lam_tmp, ones_col = cols[:, 72:73], cols[:, 73:74]
        ada_sum = work[:, 6 * D:8 * D]
        stat = sb("stat", [P, 96])
        neg_max, row_sum, inv_sum = stat[:, 0:16], stat[:, 16:32], stat[:, 32:48]
        ratio, ms, rstd, half = stat[:, 48:56], stat[:, 56:64], stat[:, 64:72], stat[:, 72:73]
        sum_sq = stat[:, 80:88]
        rb = sb("rb", [4, N_BUCKETS])
        rv = sb("rv", [4, 384])
        toeplitz = nc.dram_tensor("toeplitz", (4, 384), F32, kind="Internal")

        z = [psum(f"z{j}", [P, 1024]) for j in range(2)]
        tp = [psum(f"tp{j}", [P, 4, P]) for j in range(2)]
        oo = psum("oo", [P, 512])
        pp = psum("pp", [P, 512])

        consts, ident_ok, ld_small, ld_rb, ld_lam, col_t, col_ok, sc_ok, lam_ok = map(
            sem, ("consts", "ident_ok", "ld_small", "ld_rb", "ld_lam", "col_t", "col_ok", "sc_ok", "lam_ok"))
        ld_ada = [sem(f"ld_ada{j}") for j in range(6)]
        ld_x = [sem(f"ld_x{j}") for j in range(4)]
        sig_c, ada_used, mod_mm, mod_ok, rv_ok, st_rv, dve_pro = map(
            sem, ("sig_c", "ada_used", "mod_mm", "mod_ok", "rv_ok", "st_rv", "dve_pro"))
        x_sq, x_ms, x_rs, x_scaled, xt_done, xt_free, h_hi_ok, h_ok = map(
            sem, ("x_sq", "x_ms", "x_rs", "x_scaled", "xt_done", "xt_free", "h_hi_ok", "h_ok"))
        ld_w = [sem(f"ld_w{j}") for j in range(2)]
        whi_ok, wlo_ok, p_done, p_free = map(sem, ("whi_ok", "wlo_ok", "p_done", "p_free"))
        kh_ok, qh_ok, kl_ok, ql_ok, dup_ok, sg_sig, sg_ok = map(
            sem, ("kh_ok", "qh_ok", "kl_ok", "ql_ok", "dup_ok", "sg_sig", "sg_ok"))
        qk_done, z_free, keep_ok, scan_ok, w_ok, sq_ok, tg_done, tg_free, pv_done = map(
            sem, ("qk_done", "z_free", "keep_ok", "scan_ok", "w_ok", "sq_ok", "tg_done", "tg_free", "pv_done"))
        o_ok, ot_done, mixed_ok, max_ok, bias_hi_ok, bias_ok, ld_bias = map(
            sem, ("o_ok", "ot_done", "mixed_ok", "max_ok", "bias_hi_ok", "bias_ok", "ld_bias"))
        inv_ok, ratio_ok, onorm_ok, ssq_ok, ms_ok, rstd_ok = map(
            sem, ("inv_ok", "ratio_ok", "onorm_ok", "ssq_ok", "ms_ok", "rstd_ok"))
        ld_gate = [sem(f"ld_gate{j}") for j in range(4)]
        ld_bg, ld_fg, cb_ok, gate_used, gate_ok = map(sem, ("ld_bg", "ld_fg", "cb_ok", "gate_used", "gate_ok"))
        ld_xr = [sem(f"ld_xr{j}") for j in range(2)]
        mh_ok, ml_ok, y_done, yg_ok, r_ok, f_sq, f_ms, f_rs, f_ok = map(
            sem, ("mh_ok", "ml_ok", "y_done", "yg_ok", "r_ok", "f_sq", "f_ms", "f_rs", "f_ok"))
        st_out = [sem(f"st_out{j}") for j in range(2)]

        block = ctx.enter_context(nc.Block())

        def gate_tile(j):
            return st[:, j % 4 // 2, (j % 2) * 512:(j % 2 + 1) * 512]

        def w_tile_src(col):
            return w_in[0, :, bass.ds(col, P)].rearrange("(k p) n -> p k n", p=P)

        def x_evac(act, b):
            for gidx in range(2):
                act.wait_ge(xt_done, 2 * b + gidx + 1)
                nc.scalar.activation(
                    mixed[:].rearrange("p (k s) -> p k s", k=KT)[:, 4 * gidx:4 * gidx + 4, b * P:(b + 1) * P],
                    tp[gidx][:], ACT.Copy).then_inc(xt_free, 1)

        @block.sync
        def _(sp):
            def load_w(U, t, base):
                sp.dma_start(w_raw[:, t % 2], w_tile_src(base + GROUP_COL[t] + P * U)).then_inc(ld_w[t % 2], 16)

            def dup(U):
                for src, ok in ((kh, kh_ok), (kl, kl_ok)):
                    sp.wait_ge(ok, 2 * U + 2)
                    sp.dma_start(src[HD:P, 0, :].bitcast(F32), src[0:HD, 0, :].bitcast(F32)).then_inc(dup_ok, 16)
                    sp.dma_start(src[0:HD, 1, :].bitcast(F32), src[HD:P, 1, :].bitcast(F32)).then_inc(dup_ok, 16)

            def body(U, base1, base2, w2=True):
                sp.wait_ge(wlo_ok, 4 * U + 6)
                load_w(U + 1, 3, base1)
                for t in range(3):
                    if t == 2:
                        dup(U + 1)
                    if w2:
                        sp.wait_ge(wlo_ok, 4 * U + 7 + t)
                        load_w(U + 2, t, base2)

            def load_x(b):
                if b >= 4:
                    sp.wait_ge(xt_done, 2 * (b - 4) + 2)
                sp.dma_start(st[:, b % 4, :], x[0, b * P:(b + 1) * P, :]).then_inc(ld_x[b % 4], 16)

            def load_ada(j):
                if j >= 6:
                    sp.wait_ge(ada_used, j - 5)
                sp.dma_start(work[:, j % 6 * D:(j % 6 + 1) * D],
                             w_ada[0, j % KT * P:(j % KT + 1) * P, j // KT * D:(j // KT + 1) * D]
                             ).then_inc(ld_ada[j % 6], 16)

            for b in range(4):
                load_x(b)
            for j in range(KT):
                load_ada(j)
            for b in range(4, NB):
                load_x(b)
            for j in range(KT, 2 * KT):
                if j == 2 * KT - 2:
                    for t in range(2):
                        load_w(0, t, SB_COL)
                load_ada(j)
            for j in range(2, 7):
                if j == 5:
                    dup(0)
                sp.wait_ge(wlo_ok, j - 1)
                load_w(j // 4, j % 4, SB_COL)
            sp.wait_ge(rv_ok, 1)
            sp.dma_start(toeplitz.ap()[:, 0:TV], rv[:, 0:TV]).then_inc(st_rv, 16)

            with sp.Fori(0, SB_UNITS - 2) as U:
                body(U, SB_COL, SB_COL)
            body(2, SB_COL, -512)
            body(3, -512, -512)
            sp.wait_ge(w_ok, n(16 * SB_UNITS))
            sp.wait_ge(st_rv, 16)
            for h in range(4):
                sp.dma_start(stick[:, h * 256:(h + 1) * 256],
                             bass.AP(toeplitz, h * 384, [[1, P], [1, 256]])).then_inc(ld_bias, 16)
            with sp.Fori(4, 6) as U:
                body(U, -512, -512)
            body(6, -512, -512, w2=False)

            for k in range(KT):
                sp.wait_ge(wlo_ok, 31 + k)
                sp.dma_start(w_raw[:, k % 2].rearrange("p k n -> p (k n)"),
                             w_out[0, k * P:(k + 1) * P, :]).then_inc(ld_w[k % 2], 16)
                for j in (2 * k, 2 * k + 1):
                    if j >= 4:
                        sp.wait_ge(gate_used, j - 3)
                    else:
                        sp.wait_ge(ql_ok, 16)
                    sp.dma_start(gate_tile(j), w_ada[0, (j % 8) * P:(j % 8 + 1) * P,
                                                     2 * D + j // 8 * 512:2 * D + (j // 8 + 1) * 512]
                                 ).then_inc(ld_gate[j % 4], 16)
                if k == 2:
                    sp.wait_ge(sg_ok, 8)
                    sp.dma_start(st[:, G_, :], b_ada[:, 2 * D:3 * D].to_broadcast([P, D])).then_inc(ld_bg, 16)
            sp.wait_ge(bias_ok, 4)
            sp.dma_start(stick[:, 0:D], final_g.rearrange("(a n) -> a n", a=1).to_broadcast([P, D])).then_inc(ld_fg, 16)
            sp.wait_ge(w_ok, n(96))
            sp.wait_ge(tg_done, n(Unit(UNITS, False).tg))
            for b in range(2):
                sp.dma_start(prob[b], x[0, b * P:(b + 1) * P, :]).then_inc(ld_xr[b], 16)
            for b in range(NB):
                sp.wait_ge(f_ok, b + 1)
                sp.dma_start(out[0, b * P:(b + 1) * P, :], wT[b % 2]).then_inc(st_out[b % 2], 16)
                if b + 2 < NB:
                    sp.wait_ge(r_ok, b + 1)
                    sp.dma_start(prob[b % 2], x[0, (b + 2) * P:(b + 3) * P, :]).then_inc(ld_xr[b % 2], 16)
            for j in range(2):
                sp.wait_ge(st_out[j], 16 * NB // 2)

        @block.gpsimd
        def _(pool):
            g = nc.gpsimd
            g.memset(ident[:], 0.0).then_inc(consts, 1)
            g.memset(mask_bf[:], 0.0).then_inc(consts, 1)
            g.memset(half, -0.5).then_inc(consts, 1)
            pool.wait_ge(consts, 3)
            g.affine_select(out=ident[:], in_=ident[:], compare_op=ALU.not_equal, fill=1.0, base=0,
                            pattern=[[-1, P]], channel_multiplier=1).then_inc(ident_ok, 1)
            g.affine_select(out=mask_bf[:], in_=mask_bf[:], compare_op=ALU.is_gt, fill=NEG, base=0,
                            pattern=[[-1, P]], channel_multiplier=1).then_inc(ident_ok, 1)

            def split_lo(j, t):
                pool.wait_ge(whi_ok, j + 1)
                g.tensor_tensor(w_lo[:, t % 2], w_raw[:, t % 2], w_hi[:, t % 2], ALU.subtract).then_inc(wlo_ok, 1)

            for b in range(NB):
                pool.wait_ge(x_ms, b + 1)
                g.tensor_tensor(rstd[:, b:b + 1], ms[:, b:b + 1], half, ALU.pow).then_inc(x_rs, 1)
            for t in range(5):
                split_lo(t, t % 4)

            def body(U, sbk, w1=True, w2=True):
                un = Unit(U, sbk)
                ready = split_points(w1, w2)
                for t in range(SB_SLOTS if sbk else DA_SLOTS):
                    if not sbk and t % 2 == 0 and 6 <= t:
                        b = (t - 6) // 2
                        pool.wait_ge(ms_ok, 8 * un.da + b + 1)
                        g.tensor_tensor(rstd[:, b:b + 1], ms[:, b:b + 1], half, ALU.pow).then_inc(rstd_ok, 1)
                    for j in ready.get(t, ()):
                        split_lo(4 * U + 4 + j, j % 4)
                    if not w1 and t % 2 and 0 < t < 16:
                        out_lo(t // 2)

            def out_lo(k):
                pool.wait_ge(whi_ok, 33 + k)
                g.tensor_tensor(h_lo[:, k, :], w_raw[:, k % 2].rearrange("p k n -> p (k n)"),
                                h_hi[:, k, :], ALU.subtract).then_inc(wlo_ok, 1)

            with pool.Fori(0, SB_UNITS) as U:
                body(U, True)
            with pool.Fori(4, 6) as U:
                body(U, False)
            body(6, False, w2=False)
            body(7, False, False, False)
            for b in range(NB):
                pool.wait_ge(f_ms, b + 1)
                g.tensor_tensor(rstd[:, b:b + 1], ms[:, b:b + 1], half, ALU.pow).then_inc(f_rs, 1)

        @block.scalar
        def _(act):
            s = nc.scalar
            for sem_ in (p_free, z_free, tg_free):
                act.sem_inc(sem_, 1)
            for row, src in ((0, c), (8, norm_g), (16, b_ada[:, 0:2 * D]), (32, subln_g)):
                src = src.rearrange("a (k p) -> (a k) p", p=P)
                act.dma_start(sq_sb[row:row + src.shape[0], :], src).then_inc(ld_small, 16)
            for j, v in enumerate((lq1, lk1, lq2, lk2)):
                act.dma_start(sg[:, j * HD:(j + 1) * HD], v.to_broadcast([P, HD])).then_inc(ld_lam, 16)
            with nc.allow_non_contiguous_dma(reason="a table of 4 x 32 values"):
                act.dma_start(rb[:, :], rel_bias.rearrange("b h -> h b")).then_inc(ld_rb, 16)
            act.wait_ge(col_ok, 1)
            s.activation(sc_col, c_col, ACT.Sigmoid).then_inc(sig_c, 1)
            for b in range(NB):
                act.wait_ge(ld_x[b % 4], 16 * (b // 4 + 1))
                if b:
                    act.wait_ge(x_sq, b)
                s.activation(vv[:].rearrange("p a b -> p (a b)"), st[:, b % 4, :], ACT.Square,
                             accum_out=sum_sq[:, b:b + 1]).then_inc(x_sq, 1)
                if b:
                    x_evac(act, b - 1)
            x_evac(act, NB - 1)
            act.wait_ge(lam_ok, 2)
            s.activation(lam_exp, lam_dot, ACT.Exp).then_inc(sig_c, 1)
            act.wait_ge(mod_ok, 1)
            act.wait_ge(xt_free, 2 * NB)
            for k in range(KT):
                s.activation(h_hi[:, k, :], mixed[:, k * S:(k + 1) * S], ACT.Identity,
                             bias=mod_col[:, k:k + 1], scale=a_col[:, k:k + 1]).then_inc(h_hi_ok, 1)

            def p_evac(U1, t, c_, st_free, bank=None):
                act.wait_ge(p_done, n(8 * U1 + 2 * t + c_ + 1))
                for sem_, v in st_free:
                    act.wait_ge(sem_, v)
                s.activation(st[:, t, c_ * 512:(c_ + 1) * 512], pp[:] if bank is None else bank, ACT.Copy,
                             scale=HD ** -0.5 if t == Q_ else 1.0).then_inc(p_free, 1)

            for t in range(4):
                for c_ in range(2):
                    p_evac(0, t, c_, ((xt_done, 2 * NB),), z[t][:, c_ * 512:(c_ + 1) * 512] if t < 2 else pp[:])

            def t_evac(un, index, dst, j0, cnt, wait=()):
                act.wait_ge(tg_done, n(un.tg + index + 1))
                for sem_, v in wait:
                    act.wait_ge(sem_, v)
                s.activation(dst[:, j0 * P:(j0 + cnt) * P], tp[index % 2][:, 0:cnt, :].rearrange("p a b -> p (a b)"),
                             ACT.Copy).then_inc(tg_free, 1)

            def commit(U):
                act.wait_ge(qk_done, n(16 * U))
                act.wait_ge(p_free, n(8 * U + 4))
                s.activation(kh[0:HD, 0, :], st[0:HD, K_, :], ACT.Copy).then_inc(kh_ok, 1)
                s.activation(kh[HD:P, 1, :], st[HD:P, K_, :], ACT.Copy).then_inc(kh_ok, 1)
                s.activation(qs[0:HD, 0, :], st[0:HD, Q_, :], ACT.Copy).then_inc(qh_ok, 1)
                s.activation(qs[HD:P, 1, :], st[HD:P, Q_, :], ACT.Copy).then_inc(qh_ok, 1)

            def body(U, sbk, w1=True):
                un = Unit(U, sbk)
                vflat = vv[:].rearrange("p a b -> p (a b)")

                def evac_next(pieces):
                    for t, c_ in groups_ending(pieces):
                        free = {K_: ((kl_ok, 2 * U + 2),), Q_: ((ql_ok, 2 * U + 2),),
                                V_: ((tg_done, n(un.tg + 2)),), G_: ((sg_ok, U + 1),)}[t]
                        p_evac(U + 1, t, c_, free)

                t_evac(un, 0, vflat, 0, 4, ((pv_done, n(un.w)),))
                t_evac(un, 1, vflat, 4, 4)
                if w1:
                    evac_next(range(HEAD_PIECES))
                for t in range(SB_SLOTS if sbk else DA_SLOTS):
                    if t < 16:
                        i, m = STEPS[t]
                        L = (i + 1) * P
                        if sbk:
                            act.wait_ge(qk_done, n(un.qk + t + 1))
                            act.wait_ge(tg_done, n(un.transposed(t - 2) if t >= 3 else un.tg))
                            s.activation(prob[t % 3][:, 0:L], z[t % 2][:, 0:L], ACT.Sigmoid,
                                         scale=-1.0).then_inc(keep_ok, 1)
                            act.wait_ge(w_ok, n(un.w + (t - 1 if t >= 2 else 0)))
                            s.activation(beta[t % 2][:, 0:L], z[t % 2][:, 0:L], ACT.Sigmoid).then_inc(z_free, 1)
                        else:
                            b = t // 2
                            act.wait_ge(max_ok, 16 * un.da + t + 1)
                            if m == 0:
                                act.wait_ge(tg_done, n(un.transposed(b - 1) if b >= 2 else un.tg))
                            else:
                                act.wait_ge(w_ok, n(un.w + (b - 1 if b >= 2 else 0)))
                            dst = prob[b % 2] if m == 0 else beta[b % 2]
                            s.activation(dst[:, 0:L], z[t % 2][:, 0:L], ACT.Exp, bias=neg_max[:, t:t + 1],
                                         accum_out=row_sum[:, t:t + 1]).then_inc(z_free, 1)
                    if t == 1:
                        act.wait_ge(mixed_ok, n(un.mixed))
                        act.wait_ge(p_free, n(8 * U + 8))
                        s.activation(sg[:], st[:, G_, :], ACT.Sigmoid).then_inc(sg_sig, 1)
                    if t == 16 and w1:
                        commit(U + 1)
                    if sbk and 2 <= t < 18:
                        evac_step(un, t - 2, STEPS[t - 2][0], sb_tgroups_before(t - 2))
                    if not sbk and t >= 3 and t % 2 and t < 18:
                        b = (t - 3) // 2
                        evac_step(un, b, ORDER[b], da_tgroups_before(b))
                    if w1:
                        evac_next(pieces_of_slot(t))

            def evac_step(un, k, i, g0):
                wait = ((pv_done, n(un.w + (k - 1 if k >= 2 else 0))),)
                for gidx, j0 in enumerate(range(0, i + 1, 4)):
                    t_evac(un, g0 + gidx, wT[k % 2], j0, min(4, i + 1 - j0), wait)

            commit(0)
            with act.Fori(0, SB_UNITS) as U:
                body(U, True)
            with act.Fori(4, 7) as U:
                body(U, False)
            body(7, False, False)

            for b in range(NB):
                act.wait_ge(r_ok, b + 1)
                if b:
                    act.wait_ge(f_sq, b)
                s.activation(prob[2], beta[b % 2], ACT.Square, accum_out=sum_sq[:, b:b + 1]).then_inc(f_sq, 1)

        @block.vector
        def _(dve):
            v = nc.vector
            for sem_ in (mixed_ok, w_ok):
                dve.sem_inc(sem_, 1)
            chain = [0]

            def link(ins):
                chain[0] += 1
                ins.then_inc(dve_pro, 1)
                dve.wait_ge(dve_pro, chain[0])

            dve.wait_ge(ident_ok, 1)
            v.tensor_copy(ident_r[:], ident[:]).then_inc(sc_ok, 1)
            v.tensor_copy(ident_bf[:], ident[:]).then_inc(sc_ok, 1)
            v.memset(ones_col, 1.0).then_inc(sc_ok, 1)
            dve.wait_ge(col_t, 1)
            v.tensor_copy(raw_col, pp[:, 0:33]).then_inc(col_ok, 1)
            dve.wait_ge(sig_c, 1)
            v.tensor_tensor(sc_col, sc_col, c_col, ALU.mult).then_inc(sc_ok, 1)
            v.tensor_scalar(gs_col, sub_col, 1.0 - LAMBDA_INIT, None, ALU.mult).then_inc(sc_ok, 1)
            dve.wait_ge(sc_ok, 4)

            def scale_x(b):
                dve.wait_ge(x_sq, b + 1)
                v.tensor_scalar(ms[:, b:b + 1], sum_sq[:, b:b + 1], 1.0 / D, EPS, ALU.mult, ALU.add).then_inc(x_ms, 1)
                dve.wait_ge(x_rs, b + 1)
                v.tensor_scalar(st[:, b % 4, :], st[:, b % 4, :], rstd[:, b:b + 1], None, ALU.mult).then_inc(x_scaled, 1)

            def add_ada(j):
                k = j % KT
                acc, tile = ada_sum[:, j // KT * D:(j // KT + 1) * D], work[:, j % 6 * D:(j % 6 + 1) * D]
                dve.wait_ge(ld_ada[j % 6], 16 * (j // 6 + 1))
                if k == 0:
                    v.tensor_scalar(acc, tile, sc_col[:, k:k + 1], None, ALU.mult).then_inc(ada_used, 1)
                else:
                    dve.wait_ge(ada_used, j)
                    v.scalar_tensor_tensor(acc, tile, sc_col[:, k:k + 1], acc, ALU.mult, ALU.add).then_inc(ada_used, 1)

            for h in range(2):
                for b in range(4 * h, 4 * h + 4):
                    scale_x(b)
                if h == 1:
                    dve.wait_ge(ld_lam, 64)
                    for j in range(2):
                        v.tensor_tensor(sg[:, 256 + j * HD:256 + (j + 1) * HD], sg[:, 2 * j * HD:(2 * j + 1) * HD],
                                        sg[:, (2 * j + 1) * HD:(2 * j + 2) * HD], ALU.mult).then_inc(dve_pro, 1)
                    chain[0] += 2
                    dve.wait_ge(dve_pro, chain[0])
                    v.tensor_reduce(lam_dot, sg[:, 256:256 + 2 * HD].rearrange("p (a b) -> p a b", a=2), AX.X,
                                    ALU.add).then_inc(lam_ok, 2)
                for j in range(KT * h, KT * h + KT):
                    add_ada(j)
            dve.wait_ge(sig_c, 2)
            link(v.tensor_scalar(lam_tmp, lam_exp[:, 1:2], -LAMBDA_INIT, None, ALU.add))
            link(v.tensor_tensor(nlam, lam_tmp, lam_exp[:, 0:1], ALU.subtract))
            for t in range(2):
                dve.wait_ge(ld_w[t], 16)
                v.tensor_copy(w_hi[:, t], w_raw[:, t]).then_inc(whi_ok, 1)
            dve.wait_ge(mod_mm, 2)
            link(v.tensor_tensor(mod_col, z[0][:, 0:16], b_col, ALU.add))
            v.scalar_tensor_tensor(a_col, mod_col[:, 8:16], 1.0, g_col, ALU.add, ALU.mult).then_inc(mod_ok, 1)
            dve.wait_ge(mod_ok, 1)

            def split_hi(U1, t):
                dve.wait_ge(ld_w[t % 2], 32 * U1 + 16 * (t // 2 + 1))
                dve.wait_ge(p_done, n(8 * U1 + 2 * t - 2))
                v.tensor_copy(w_hi[:, t % 2], w_raw[:, t % 2]).then_inc(whi_ok, 1)

            for k in range(KT):
                xk = mixed[:, k * S:(k + 1) * S]
                dve.wait_ge(h_hi_ok, k + 1)
                link(v.tensor_scalar(xk, xk, a_col[:, k:k + 1], mod_col[:, k:k + 1], ALU.mult, ALU.add))
                v.tensor_tensor(h_lo[:, k, :], xk, h_hi[:, k, :], ALU.subtract).then_inc(h_ok, 1)
            for t in range(2, 5):
                split_hi(t // 4, t % 4)
            dve.wait_ge(ld_rb, 16)
            link(v.tensor_scalar(rb[:, :], rb[:, :], rb[:, N_BUCKETS - 1:N_BUCKETS], None, ALU.subtract))
            link(v.memset(rv[:, 0:P - 1], NEG))
            for bkt, (lo, hi) in enumerate(buckets_by_distance()):
                fill = v.tensor_copy(rv[:, P - 1 + lo:P + hi], rb[:, bkt:bkt + 1].to_broadcast([4, hi - lo + 1]))
                if bkt < N_BUCKETS - 1:
                    link(fill)
            fill.then_inc(rv_ok, 1)
            v.memset(stick[:, :], 1.0).then_inc(dve_pro, 1)
            chain[0] += 1
            dve.wait_ge(dve_pro, chain[0])

            def commit(U):
                dve.wait_ge(kh_ok, 2 * U + 2)
                v.tensor_tensor(kl[0:HD, 0, :], st[0:HD, K_, :], kh[0:HD, 0, :], ALU.subtract).then_inc(kl_ok, 1)
                v.tensor_tensor(kl[HD:P, 1, :], st[HD:P, K_, :], kh[HD:P, 1, :], ALU.subtract).then_inc(kl_ok, 1)
                dve.wait_ge(qh_ok, 2 * U + 2)
                v.tensor_tensor(qs[HD:P, 0, :], st[0:HD, Q_, :], qs[0:HD, 0, :], ALU.subtract).then_inc(ql_ok, 1)
                v.tensor_tensor(qs[0:HD, 1, :], st[HD:P, Q_, :], qs[HD:P, 1, :], ALU.subtract).then_inc(ql_ok, 1)

            def body(U, sbk, w1=True, w2=True):
                un = Unit(U, sbk)
                ready = split_points(w1, w2)

                def splits(t):
                    for j in ready.get(t, ()):
                        split_hi(U + 1 + j // 4, j % 4)
                    if not w1:
                        last_unit_work(t)

                def gated(b):
                    i = ORDER[b]
                    dve.wait_ge(sg_ok, U + 1)
                    gate = sg[:, i * P:(i + 1) * P]
                    if sbk:
                        dve.wait_ge(pv_done, n(un.w + 2 * b + 2))
                        v.tensor_tensor(mixed[:, bass.ds((U + 4) * S + i * P, P)], oo[:, 0:P], gate,
                                        ALU.mult).then_inc(mixed_ok, 1)
                    else:
                        dve.wait_ge(ot_done, n(8 * un.da + b + 1))
                        v.scalar_tensor_tensor(mixed[:, bass.ds((U - 4) * S + i * P, P)],
                                               oo[:, P:2 * P], gs_col, gate, ALU.mult, ALU.mult).then_inc(mixed_ok, 1)

                if not sbk:
                    dve.wait_ge(qk_done, n(un.qk))
                    dve.wait_ge(ld_bias, 64)
                    braw = stick[:, bass.ds(un.da * 256, 256)]
                    v.tensor_copy(bias_hi[:, ::-1], braw).then_inc(bias_hi_ok, 1)
                    dve.wait_ge(bias_hi_ok, un.da + 1)
                    v.tensor_tensor(bias_lo[:, ::-1], braw, bias_hi[:, ::-1], ALU.subtract).then_inc(bias_ok, 1)
                splits(-1)
                for t in range(SB_SLOTS if sbk else DA_SLOTS):
                    L = (STEPS[t][0] + 1) * P if t < 16 else 0
                    if sbk:
                        if t >= 5 and t % 2:
                            gated((t - 5) // 2)
                        if t < 16:
                            dve.wait_ge(keep_ok, un.qk + t + 1)
                            dve.wait_ge(w_ok, n(un.w + t))
                            kp = prob[t % 3][:, 0:L][:, ::-1]
                            v.tensor_tensor_scan(stick[:, 0:L][:, ::-1], kp, kp, 1.0,
                                                 ALU.mult, ALU.bypass).then_inc(scan_ok, 1)
                        if t < 16:
                            dve.wait_ge(z_free, n(un.qk + t + 1))
                            dve.wait_ge(scan_ok, un.qk + t + 1)
                            v.tensor_tensor(prob[t % 3][:, 0:L], beta[t % 2][:, 0:L], stick[:, 1:L + 1],
                                            ALU.mult).then_inc(w_ok, 1)
                    else:
                        leaves = t % 2 == 0 and 6 <= t
                        if leaves:
                            da_leave_1(un, (t - 6) // 2)
                        if t < 16:
                            dve.wait_ge(qk_done, n(un.qk + t + 1))
                            v.tensor_reduce(neg_max[:, t:t + 1], z[t % 2][:, 0:L], AX.X, ALU.max,
                                            negate=True).then_inc(max_ok, 1)
                        if leaves:
                            da_leave_2(un, (t - 6) // 2)
                        if t >= 2 and t % 2 == 0 and t <= 16:
                            combine(un, t // 2 - 1)
                        if leaves:
                            gated((t - 6) // 2)
                    if t == 3:
                        dve.wait_ge(sg_sig, U + 1)
                        v.tensor_tensor(sg[:], sg[:], st[:, G_, :], ALU.mult).then_inc(sg_ok, 1)
                    if t == 16 and w1:
                        commit(U + 1)
                    splits(t)

            def last_unit_work(t):
                if t == -1:
                    dve.wait_ge(tg_done, n(Unit(7, False).tg + 2))
                    for j in range(KT):
                        v.tensor_scalar(st[:, V_, j * P:(j + 1) * P], ident[:], 0.0, sc_col[:, j:j + 1],
                                        ALU.mult, ALU.add).then_inc(cb_ok, 1)
                if t % 2 and 0 < t < 16:
                    k = t // 2
                    dve.wait_ge(ld_w[k % 2], 16 * (16 + k // 2 + 1))
                    v.tensor_copy(h_hi[:, k, :], w_raw[:, k % 2].rearrange("p k n -> p (k n)")).then_inc(whi_ok, 1)
                if t in (8, 16):
                    half_ = slice((t // 16) * 512, (t // 16 + 1) * 512)
                    dve.wait_ge(gate_used, t)
                    dve.wait_ge(ld_bg, 16)
                    v.tensor_tensor(st[:, G_, half_], pp[:], st[:, G_, half_], ALU.add).then_inc(gate_ok, 1)

            def combine(un, b):
                i = ORDER[b]
                L = (i + 1) * P
                t0 = 2 * b
                dve.wait_ge(z_free, n(un.qk + t0 + 2))
                v.reciprocal(inv_sum[:, t0:t0 + 2], row_sum[:, t0:t0 + 2]).then_inc(inv_ok, 1)
                dve.wait_ge(inv_ok, 8 * un.da + b + 1)
                v.tensor_scalar(ratio[:, b:b + 1], row_sum[:, t0:t0 + 1], inv_sum[:, t0 + 1:t0 + 2], nlam,
                                ALU.mult, ALU.mult).then_inc(ratio_ok, 1)
                dve.wait_ge(ratio_ok, 8 * un.da + b + 1)
                v.scalar_tensor_tensor(prob[b % 2][:, 0:L], beta[b % 2][:, 0:L], ratio[:, b:b + 1],
                                       prob[b % 2][:, 0:L], ALU.mult, ALU.add).then_inc(w_ok, 1)

            def da_leave_1(un, b):
                dve.wait_ge(pv_done, n(un.w + b + 1))
                dve.wait_ge(ot_done, n(8 * un.da + b))
                v.tensor_scalar(o_sb[:], oo[:, 0:P], inv_sum[:, 2 * b:2 * b + 1], None, ALU.mult).then_inc(onorm_ok, 1)
                dve.wait_ge(onorm_ok, 8 * un.da + b + 1)
                v.tensor_tensor(sq_sb[:], o_sb[:], o_sb[:], ALU.mult).then_inc(sq_ok, 1)
                dve.wait_ge(sq_ok, 8 * un.da + b + 1)
                v.tensor_reduce(sum_sq[:, b:b + 1], sq_sb[:], AX.X, ALU.add).then_inc(ssq_ok, 1)
                dve.wait_ge(ssq_ok, 8 * un.da + b + 1)
                v.tensor_scalar(ms[:, b:b + 1], sum_sq[:, b:b + 1], 1.0 / P, EPS, ALU.mult, ALU.add).then_inc(ms_ok, 1)

            def da_leave_2(un, b):
                dve.wait_ge(rstd_ok, 8 * un.da + b + 1)
                v.tensor_scalar(o_sb[:], o_sb[:], rstd[:, b:b + 1], None, ALU.mult).then_inc(o_ok, 1)

            commit(0)
            with dve.Fori(0, SB_UNITS) as U:
                body(U, True)
            with dve.Fori(4, 6) as U:
                body(U, False)
            body(6, False, w2=False)
            body(7, False, False, False)

            mT = mixed[:].rearrange("p (k s) -> p k s", k=KT)

            def split_mixed(b):
                if b >= 2:
                    dve.wait_ge(y_done, b - 1)
                v.tensor_copy(w_hi[:, b % 2], mT[:, :, b * P:(b + 1) * P]).then_inc(mh_ok, 1)
                dve.wait_ge(mh_ok, b + 1)
                v.tensor_tensor(w_lo[:, b % 2], mT[:, :, b * P:(b + 1) * P], w_hi[:, b % 2],
                                ALU.subtract).then_inc(ml_ok, 1)

            def final_scale(b):
                dve.wait_ge(f_sq, b + 1)
                v.tensor_scalar(ms[:, b:b + 1], sum_sq[:, b:b + 1], 1.0 / D, EPS, ALU.mult, ALU.add).then_inc(f_ms, 1)
                dve.wait_ge(f_rs, b + 1)
                if b >= 2:
                    dve.wait_ge(st_out[b % 2], 16 * (b // 2))
                v.scalar_tensor_tensor(wT[b % 2], beta[b % 2], rstd[:, b:b + 1], stick[:, 0:D],
                                       ALU.mult, ALU.mult).then_inc(f_ok, 1)

            dve.wait_ge(mixed_ok, n(64))
            dve.wait_ge(p_done, n(64))
            split_mixed(0)
            dve.wait_ge(ld_fg, 16)
            for b in range(NB):
                if b + 1 < NB:
                    split_mixed(b + 1)
                dve.wait_ge(y_done, b + 1)
                if b >= 2:
                    dve.wait_ge(f_ok, b - 1)
                v.tensor_tensor(beta[b % 2], z[b % 2][:, :], st[:, G_, :], ALU.mult).then_inc(yg_ok, 1)
                dve.wait_ge(yg_ok, b + 1)
                dve.wait_ge(ld_xr[b % 2], 16 * (b // 2 + 1))
                v.tensor_tensor(beta[b % 2], beta[b % 2], prob[b % 2], ALU.add).then_inc(r_ok, 1)
                if b:
                    final_scale(b - 1)
            final_scale(NB - 1)

        @block.tensor
        def _(pe):
            t_ = nc.tensor
            for sem_ in (p_done, qk_done, tg_done, pv_done, ot_done):
                pe.sem_inc(sem_, 1)

            def transpose_x(b):
                pe.wait_ge(x_scaled, b + 1)
                for gidx in range(2):
                    if b:
                        pe.wait_ge(xt_free, 2 * b + gidx - 1)
                    for j in range(4):
                        k = 4 * gidx + j
                        tr = t_.transpose(tp[gidx][:, j, :], st[:, b % 4, k * P:(k + 1) * P], ident[:])
                    tr.then_inc(xt_done, 1)

            pe.wait_ge(ident_ok, 2)
            pe.wait_ge(ld_small, 64)
            t_.transpose(pp[:, 0:33], sq_sb[0:33, :], ident[0:33, 0:33]).then_inc(col_t, 1)
            pe.wait_ge(sc_ok, 4)
            for h in range(2):
                for b in range(4 * h, 4 * h + 4):
                    transpose_x(b)
                pe.wait_ge(ada_used, KT * (h + 1))
                for j in range(KT * h, KT * h + KT):
                    mm = t_.matmul(z[0][:, j:j + 1], ada_sum[:, j * P:(j + 1) * P], ones_col,
                                   start=j == 0, stop=True, skip_group_check=True)
                mm.then_inc(mod_mm, 1)

            def piece(U1, p, first=False):
                t, c_, pas = p // 6, p % 6 // 3, p % 3
                if p % 6 == 0:
                    pe.wait_ge(wlo_ok, 4 * U1 + t + 1)
                if pas == 0 and not first:
                    pe.wait_ge(p_free, n(8 * U1 + 2 * t + c_))
                lhs = w_lo if pas == 2 else w_hi
                rhs = h_lo if pas == 1 else h_hi
                for k in range(KT):
                    mm = t_.matmul(pp[:], lhs[:, t % 2, k, :], rhs[:, k, c_ * 512:(c_ + 1) * 512],
                                   start=(pas == 0 and k == 0), stop=(pas == 2 and k == KT - 1))
                if pas == 2:
                    mm.then_inc(p_done, 1)

            pe.wait_ge(wlo_ok, 2)
            for k in range(KT):
                pe.wait_ge(h_ok, k + 1)
                for t in range(2):
                    for c_ in range(2):
                        for pas in range(3):
                            mm = t_.matmul(z[t][:, c_ * 512:(c_ + 1) * 512], (w_lo if pas == 2 else w_hi)[:, t, k, :],
                                           (h_lo if pas == 1 else h_hi)[:, k, c_ * 512:(c_ + 1) * 512],
                                           start=(pas == 0 and k == 0), stop=(pas == 2 and k == KT - 1))
                        if k == KT - 1:
                            mm.then_inc(p_done, 1)
            for p in range(12, PIECES):
                piece(0, p, p == 12)

            def logits(un, t):
                i, m = STEPS[t]
                L = (i + 1) * P
                pe.wait_ge(z_free, n(un.qk + (t - 1 if t >= 2 else 0)))
                for ch in range(0, L, 512):
                    e = min(ch + 512, L)
                    q = qs[:, m, i * P:(i + 1) * P]
                    if un.sb:
                        adds = [(ident_bf, mask_bf, i * P, (i + 1) * P, 0)]
                    else:
                        adds = [(ident_r, bb, lo, hi, (1 - i) * P) for bb in (bias_hi, bias_lo)
                                for lo, hi in [(max(i - 1, 0) * P, (i + 1) * P)]]
                    adds = [(a, bb, max(lo, ch), min(hi, e), off) for a, bb, lo, hi, off in adds if max(lo, ch) < min(hi, e)]
                    t_.matmul(z[t % 2][:, ch:e], q, kh[:, m, ch:e], start=True, stop=False)
                    mm = t_.matmul(z[t % 2][:, ch:e], q, kl[:, m, ch:e], start=False, stop=not adds)
                    for x_, (a, bb, lo, hi, off) in enumerate(adds):
                        if un.sb:
                            mm = t_.matmul(z[t % 2][:, lo:hi], a[:], bb[:], start=False, stop=True)
                        else:
                            mm = t_.matmul(z[t % 2][:, lo:hi], a[:], bb[:, lo + off:hi + off], start=False,
                                           stop=x_ == len(adds) - 1)
                mm.then_inc(qk_done, 1)

            def transposes(un, k, i, src, g0):
                pe.wait_ge(w_ok, n(un.w + k + 1))
                for gidx, j0 in enumerate(range(0, i + 1, 4)):
                    pe.wait_ge(tg_free, n(un.tg + g0 + gidx - 1))
                    for j in range(j0, min(j0 + 4, i + 1)):
                        tr = t_.transpose(tp[(g0 + gidx) % 2][:, j - j0, :], src[:, j * P:(j + 1) * P], ident[:])
                    tr.then_inc(tg_done, 1)

            def values(un, k, i, b, m):
                pe.wait_ge(tg_free, n(un.transposed(k + 1)))
                if not m:
                    pe.wait_ge(mixed_ok, n(un.mixed + b))
                for j in range(i + 1):
                    wt = wT[k % 2][:, j * P:(j + 1) * P]
                    if m is None:
                        mm = t_.matmul(oo[:, 0:P], wt, vv[:, j, :], start=j == 0, stop=j == i)
                    else:
                        mm = t_.matmul(oo[m * HD:(m + 1) * HD, 0:P], vv[:, j, m * HD:(m + 1) * HD], wt,
                                       start=j == 0, stop=j == i)
                mm.then_inc(pv_done, 1)

            def body(U, sbk, w1=True):
                un = Unit(U, sbk)
                pe.wait_ge(p_free, n(8 * U + 6))
                for gidx in range(2):
                    pe.wait_ge(tg_free, n(un.tg))
                    for j in range(4):
                        tr = t_.transpose(tp[gidx][:, j, :], st[:, V_, (4 * gidx + j) * P:(4 * gidx + j + 1) * P], ident[:])
                    tr.then_inc(tg_done, 1)
                if w1:
                    for p in range(HEAD_PIECES):
                        piece(U + 1, p)
                pe.wait_ge(ql_ok, 2 * U + 2)
                pe.wait_ge(dup_ok, 64 * U + 64)
                pe.wait_ge(kl_ok, 2 * U + 2)
                if not sbk:
                    pe.wait_ge(bias_ok, un.da + 1)
                for t in range(SB_SLOTS if sbk else DA_SLOTS):
                    if t < 16:
                        logits(un, t)
                    if sbk and 2 <= t < 18:
                        transposes(un, t - 2, STEPS[t - 2][0], prob[(t - 2) % 3], sb_tgroups_before(t - 2))
                    ps = list(pieces_of_slot(t)) if w1 else []
                    for p in ps[:1]:
                        piece(U + 1, p)
                    for p in ps[1:]:
                        piece(U + 1, p)
                    if not sbk and t % 2 == 0 and 6 <= t:
                        b = (t - 6) // 2
                        pe.wait_ge(o_ok, 8 * un.da + b + 1)
                        t_.transpose(oo[:, P:2 * P], o_sb[:], ident[:]).then_inc(ot_done, 1)
                    if not w1 and t < 16:
                        gate_product(t)
                    if sbk and 3 <= t < 19:
                        values(un, t - 3, STEPS[t - 3][0], (t - 3) // 2, (t - 3) % 2)
                    if not sbk and t % 2 and 3 <= t < 18:
                        b = (t - 3) // 2
                        transposes(un, b, ORDER[b], prob[b % 2], da_tgroups_before(b))
                    if not sbk and t % 2 and 5 <= t < 20:
                        values(un, (t - 5) // 2, ORDER[(t - 5) // 2], (t - 5) // 2, None)

            def gate_product(j):
                if j == 0:
                    pe.wait_ge(cb_ok, KT)
                    pe.wait_ge(p_free, n(64))
                if j == 8:
                    pe.wait_ge(gate_ok, 1)
                pe.wait_ge(ld_gate[j % 4], 16 * (j // 4 + 1))
                t_.matmul(pp[:], st[:, V_, (j % 8) * P:(j % 8 + 1) * P], gate_tile(j),
                          start=j % 8 == 0, stop=j % 8 == 7).then_inc(gate_used, 1)

            with pe.Fori(0, SB_UNITS) as U:
                body(U, True)
            with pe.Fori(4, 7) as U:
                body(U, False)
            body(7, False, False)

            pe.wait_ge(wlo_ok, 40)
            pe.wait_ge(z_free, n(128))
            for b in range(NB):
                pe.wait_ge(ml_ok, b + 1)
                if b >= 2:
                    pe.wait_ge(yg_ok, b - 1)
                for ch in range(2):
                    for pas in range(3):
                        lhs, rhs = (w_lo if pas == 2 else w_hi), (h_lo if pas == 1 else h_hi)
                        for k in range(KT):
                            mm = t_.matmul(z[b % 2][:, ch * 512:(ch + 1) * 512], lhs[:, b % 2, k, :],
                                           rhs[:, k, ch * 512:(ch + 1) * 512],
                                           start=(pas == 0 and k == 0), stop=(pas == 2 and k == KT - 1))
                mm.then_inc(y_done, 1)


_INS = ["x", "c", "norm_g", "w_ada", "b_ada", "w_in", "lambda_q1", "lambda_k1", "lambda_q2", "lambda_k2",
        "subln_g", "w_out", "rel_bias", "final_g"]


def kernel(**inputs):
    import numpy as _np
    import concourse.bacc as _bacc
    from concourse.bass_utils import run_bass_kernel_spmd as _run

    nc = _bacc.Bacc("TRN2", target_bir_lowering=False, num_devices=1)
    arrays, args = {}, []
    for name in _INS:
        a = _np.ascontiguousarray(inputs[name])
        arrays[f"in_{name}_dram"] = a
        args.append(nc.dram_tensor(f"in_{name}_dram", a.shape, mybir.dt.from_np(a.dtype), kind="ExternalInput").ap())
    out = nc.dram_tensor("out_0_dram", (1, S, D), F32, kind="ExternalOutput").ap()
    layer_kernel(nc, *args, out)
    r = _run(nc, [arrays], core_ids=[0])
    return r.results[0]["out_0_dram"]
```

```python
import math
from contextlib import ExitStack

import concourse.bass as bass
from concourse import mybir
from concourse.alu_op_type import AluOpType as ALU

F32 = mybir.dt.float32
F32R = mybir.dt.float32r
BF16 = mybir.dt.bfloat16
ACT = mybir.ActivationFunctionType
AX = mybir.AxisListType

P = 128
D = 1024
S = 1024
NB = S // P
KT = D // P
HD = 64
UNITS = 8
SB_UNITS = 4
EPS = 1e-6
NEG = -1e30
LAMBDA_INIT = 0.8 - 0.6 * math.exp(-0.3 * 0)
N_BUCKETS = 32
MAX_DISTANCE = 128
TV = 383

K_, Q_, V_, G_ = range(4)
GROUP_COL = {K_: 512, Q_: 0, V_: 1024, G_: 1536}
SB_COL = 2048

ORDER = [7, 6, 5, 4, 3, 2, 1, 0]
STEPS = [(i, m) for i in ORDER for m in range(2)]
HEAD_PIECES = 3
SB_SLOTS, DA_SLOTS = 20, 21
SB_TAIL = (2, 2, 1, 0)
DA_TAIL = (1, 1, 1, 1, 1)
PIECES = 24


def pieces_of_slot(t, sb=True):
    tail = SB_TAIL if sb else DA_TAIL
    rest = PIECES - HEAD_PIECES - sum(tail)
    if t >= 16:
        lo = HEAD_PIECES + rest + sum(tail[:t - 16])
        return range(lo, lo + tail[t - 16])
    lo, hi = rest * t // 16, rest * (t + 1) // 16
    return range(HEAD_PIECES + lo, HEAD_PIECES + hi)


def split_points(w1=True, w2=True):
    done = {p: t for t in range(SB_SLOTS) for p in pieces_of_slot(t)}
    pts = {}
    if w1:
        pts.setdefault(0, []).append(1)
        pts.setdefault(done[5] + 1, []).append(2)
        pts.setdefault(done[11] + 1, []).append(3)
    if w2:
        pts.setdefault(done[17] + 1, []).append(4)
    return pts


LAST = 3
OUT_TILES = [k for k in range(KT) if k != LAST] + [LAST]
LO_POOL = (0, 4)
CHUNKS = 2 * NB
FIRST_CHUNK = 3


def groups_ending(pieces):
    return [(p // 6, (p % 6) // 3) for p in pieces if p % 3 == 2]


def buckets_by_distance():
    exact = N_BUCKETS // 2
    out = []
    for n in range(256):
        b = n if n < exact else min(
            N_BUCKETS - 1, exact + int(math.log(n / exact) / math.log(MAX_DISTANCE / exact) * (N_BUCKETS - exact)))
        if b < len(out):
            out[b][1] = n
        else:
            while len(out) < b:
                out.append(None)
            out.append([n, n])
    return out


def n(count):
    return count + 1


def sb_tgroups_before(step):
    return 2 + sum((STEPS[s][0] + 4) // 4 for s in range(step))


def da_tgroups_before(b):
    return 2 + sum((ORDER[j] + 4) // 4 for j in range(b))


SB_TG = sb_tgroups_before(16)
DA_TG = da_tgroups_before(8)


class Unit:

    def __init__(self, U, sb):
        self.U, self.sb = U, sb
        self.qk = 16 * U
        self.mixed = 8 * U
        self.w = 16 * U if sb else 8 * U + 32
        self.tg = SB_TG * U if sb else DA_TG * U + (SB_UNITS * (SB_TG - DA_TG))
        self.da = None if sb else U - SB_UNITS

    def transposed(self, steps):
        return self.tg + (sb_tgroups_before(steps) if self.sb else da_tgroups_before(steps))


def layer_kernel(nc, x, c, norm_g, w_ada, b_ada, w_in, lq1, lk1, lq2, lk2, subln_g, w_out, rel_bias, final_g, out):
    ctx = ExitStack()
    with ctx:
        def sb(name, shape, dt=F32):
            return ctx.enter_context(nc.sbuf_tensor(name, shape, dt))

        def psum(name, shape):
            return ctx.enter_context(nc.psum_tensor(name, shape, F32))

        def sem(name):
            return ctx.enter_context(nc.semaphore(name))

        h_hi = sb("h_hi", [P, KT, S], F32R)
        h_lo = sb("h_lo", [P, KT, S], F32R)
        mixed = sb("mixed", [P, KT * S])
        st = sb("st", [P, 4, S])
        qs = sb("qs", [P, 2, S], F32R)
        kh = sb("kh", [P, 2, S], F32R)
        kl = sb("kl", [P, 2, S], F32R)
        vv = sb("vv", [P, NB, P])
        sg = sb("sg", [P, S])
        w_raw = sb("w_raw", [P, 2, KT, P])
        w_hi = sb("w_hi", [P, 2, KT, P], F32R)
        w_lo = sb("w_lo", [P, 2, KT, P], F32R)
        work = sb("work", [P, 8256])
        prob = [work[:, j * 1024:(j + 1) * 1024] for j in range(3)]
        beta = [work[:, (3 + j) * 1024:(4 + j) * 1024] for j in range(2)]
        wT = [work[:, (5 + j) * 1024:(6 + j) * 1024] for j in range(2)]
        stick = work[:, 7 * 1024:7 * 1024 + 1032]
        o_sb = sb("o_sb", [P, P])
        sq_sb = sb("sq_sb", [P, P])
        bias_hi = sb("bias_hi", [P, 256], F32R)
        bias_lo = sb("bias_lo", [P, 256], F32R)
        ident = sb("ident", [P, P])
        ident_r = sb("ident_r", [P, P], F32R)
        ident_bf = sb("ident_bf", [P, P], BF16)
        mask_bf = sb("mask_bf", [P, P], BF16)
        cols = sb("cols", [P, 96])
        raw_col = cols[:, 0:33]
        c_col, g_col, b_col, sub_col = cols[:, 0:8], cols[:, 8:16], cols[:, 16:32], cols[:, 32:33]
        sc_col, a_col = cols[:, 33:41], cols[:, 41:49]
        mod_col, gs_col = cols[:, 49:65], cols[:, 65:66]
        nlam, lam_dot, lam_exp = cols[:, 66:67], cols[:, 68:70], cols[:, 70:72]
        lam_tmp, ones_col = cols[:, 72:73], cols[:, 73:74]
        ada_sum = work[:, 6 * D:8 * D]
        stat = sb("stat", [P, 96])
        neg_max, row_sum, inv_sum = stat[:, 0:16], stat[:, 16:32], stat[:, 32:48]
        ratio, ms, rstd, half = stat[:, 48:56], stat[:, 56:64], stat[:, 64:72], stat[:, 72:73]
        sum_sq = stat[:, 80:88]
        rb = sb("rb", [4, N_BUCKETS])
        rv = sb("rv", [4, 384])
        toeplitz = nc.dram_tensor("toeplitz", (4, 384), F32, kind="Internal")
        gate_dram = nc.dram_tensor("gate_dram", (1, D), F32, kind="Internal")
        last_out = prob[2]
        last_hi, last_lo = kl[:, 0, :], kl[:, 1, :]
        wo_raw = [w_raw[:, 0].rearrange("p k n -> p (k n)"), w_raw[:, 1].rearrange("p k n -> p (k n)"), prob[2],
                  stick[:, 0:D]]
        gate_b, final_b = st[:, K_, :], st[:, G_, :]
        x_res = [st[:, Q_, :], st[:, V_, :]]
        out_ring = [prob[0], prob[1], beta[0], beta[1]]

        z = [psum(f"z{j}", [P, 1024]) for j in range(2)]
        tp = [psum(f"tp{j}", [P, 4, P]) for j in range(2)]
        oo = psum("oo", [P, 512])
        pp = psum("pp", [P, 512])

        consts, ident_ok, ld_small, ld_rb, ld_lam, col_t, col_ok, sc_ok, lam_ok = map(
            sem, ("consts", "ident_ok", "ld_small", "ld_rb", "ld_lam", "col_t", "col_ok", "sc_ok", "lam_ok"))
        ld_ada = [sem(f"ld_ada{j}") for j in range(6)]
        ld_x = [sem(f"ld_x{j}") for j in range(4)]
        sig_c, ada_used, mod_mm, mod_ok, rv_ok, st_rv, dve_pro = map(
            sem, ("sig_c", "ada_used", "mod_mm", "mod_ok", "rv_ok", "st_rv", "dve_pro"))
        x_sq, x_ms, x_rs, x_scaled, xt_done, xt_free, h_hi_ok, h_ok = map(
            sem, ("x_sq", "x_ms", "x_rs", "x_scaled", "xt_done", "xt_free", "h_hi_ok", "h_ok"))
        ld_w = [sem(f"ld_w{j}") for j in range(2)]
        whi_ok, wlo_ok, p_done, p_free = map(sem, ("whi_ok", "wlo_ok", "p_done", "p_free"))
        kh_ok, qh_ok, kl_ok, ql_ok, dup_ok, sg_sig, sg_ok = map(
            sem, ("kh_ok", "qh_ok", "kl_ok", "ql_ok", "dup_ok", "sg_sig", "sg_ok"))
        qk_done, z_free, keep_ok, scan_ok, w_ok, sq_ok, tg_done, tg_free, pv_done = map(
            sem, ("qk_done", "z_free", "keep_ok", "scan_ok", "w_ok", "sq_ok", "tg_done", "tg_free", "pv_done"))
        o_ok, ot_done, mixed_ok, max_ok, bias_hi_ok, bias_ok, ld_bias = map(
            sem, ("o_ok", "ot_done", "mixed_ok", "max_ok", "bias_hi_ok", "bias_ok", "ld_bias"))
        inv_ok, ratio_ok, onorm_ok, ssq_ok, ms_ok, rstd_ok = map(
            sem, ("inv_ok", "ratio_ok", "onorm_ok", "ssq_ok", "ms_ok", "rstd_ok"))
        ld_bg, gate_mm, gate_row, st_gate, ld_gate, ld_fg = map(
            sem, ("ld_bg", "gate_mm", "gate_row", "st_gate", "ld_gate", "ld_fg"))
        ld_wo = [sem(f"ld_wo{k}") for k in range(4)]
        ld_xr = [sem(f"ld_xr{j}") for j in range(2)]
        last_gated, wo_hi, wo_lo_pool, wo_lo_dve, mh_ok, ml_ok, part_done, part_free, part_ok, oh_ok, o_split = map(
            sem, ("last_gated", "wo_hi", "wo_lo_pool", "wo_lo_dve", "mh_ok", "ml_ok", "part_done", "part_free",
                  "part_ok", "oh_ok", "o_split"))
        y_done, r_ok, f_sq, f_ms, f_rs, f_ok = map(sem, ("y_done", "r_ok", "f_sq", "f_ms", "f_rs", "f_ok"))
        st_out = [sem(f"st_out{j}") for j in range(4)]

        block = ctx.enter_context(nc.Block())

        def chunk_bank(t, c_):
            if t < 2:
                return z[t][:, c_ * 512:(c_ + 1) * 512]
            return z[1][:, (t - 2) * 512:(t - 1) * 512] if c_ else pp[:]

        def mixed_block(i):
            return mixed[:].rearrange("p (k s) -> p k s", k=KT)[:, :, i * P:(i + 1) * P]

        def w_tile_src(col):
            return w_in[0, :, bass.ds(col, P)].rearrange("(k p) n -> p k n", p=P)

        def x_evac(act, b):
            for gidx in range(2):
                act.wait_ge(xt_done, 2 * b + gidx + 1)
                nc.scalar.activation(
                    mixed[:].rearrange("p (k s) -> p k s", k=KT)[:, 4 * gidx:4 * gidx + 4, b * P:(b + 1) * P],
                    tp[gidx][:], ACT.Copy).then_inc(xt_free, 1)

        @block.sync
        def _(sp):
            def load_w(U, t, base):
                sp.dma_start(w_raw[:, t % 2], w_tile_src(base + GROUP_COL[t] + P * U)).then_inc(ld_w[t % 2], 16)

            def dup(U):
                for src, ok in ((kh, kh_ok), (kl, kl_ok)):
                    sp.wait_ge(ok, 2 * U + 2)
                    sp.dma_start(src[HD:P, 0, :].bitcast(F32), src[0:HD, 0, :].bitcast(F32)).then_inc(dup_ok, 16)
                    sp.dma_start(src[0:HD, 1, :].bitcast(F32), src[HD:P, 1, :].bitcast(F32)).then_inc(dup_ok, 16)

            def body(U, base1, base2, w2=True):
                sp.wait_ge(wlo_ok, 4 * U + 6)
                load_w(U + 1, 3, base1)
                for t in range(3):
                    if t == 2:
                        dup(U + 1)
                    if w2:
                        sp.wait_ge(wlo_ok, 4 * U + 7 + t)
                        load_w(U + 2, t, base2)

            def load_x(b):
                if b >= 4:
                    sp.wait_ge(xt_done, 2 * (b - 4) + 2)
                sp.dma_start(st[:, b % 4, :], x[0, b * P:(b + 1) * P, :]).then_inc(ld_x[b % 4], 16)

            def load_ada(j):
                if j >= 6:
                    sp.wait_ge(ada_used, j - 5)
                sp.dma_start(work[:, j % 6 * D:(j % 6 + 1) * D],
                             w_ada[0, j % KT * P:(j % KT + 1) * P, j // KT * D:(j // KT + 1) * D]
                             ).then_inc(ld_ada[j % 6], 16)

            for b in range(4):
                load_x(b)
            for j in range(4):
                load_ada(j)
            for b in range(4, NB):
                load_x(b)
            for j in range(4, KT):
                load_ada(j)
            for j in range(KT, 2 * KT):
                if j == 2 * KT - 2:
                    for t in range(2):
                        load_w(0, t, SB_COL)
                load_ada(j)
            sp.wait_ge(lam_ok, 2)
            sp.dma_start(sg[0:1, :], b_ada[:, 2 * D:3 * D]).then_inc(ld_bg, 16)
            for j in range(2 * KT, 3 * KT - 2):
                load_ada(j)
            for j in range(2, 7):
                if j == 4:
                    for k in range(3 * KT - 2, 3 * KT):
                        load_ada(k)
                    dup(0)
                sp.wait_ge(wlo_ok, j - 1)
                load_w(j // 4, j % 4, SB_COL)
            sp.wait_ge(gate_row, 1)
            sp.dma_start(gate_dram.ap(), sg[0:1, :]).then_inc(st_gate, 16)
            sp.wait_ge(rv_ok, 1)
            sp.dma_start(toeplitz.ap()[:, 0:TV], rv[:, 0:TV]).then_inc(st_rv, 16)

            with sp.Fori(0, SB_UNITS - 2) as U:
                body(U, SB_COL, SB_COL)
            body(2, SB_COL, -512)
            body(3, -512, -512)
            sp.wait_ge(w_ok, n(16 * SB_UNITS))
            sp.wait_ge(st_rv, 16)
            for h in range(4):
                sp.dma_start(stick[:, h * 256:(h + 1) * 256],
                             bass.AP(toeplitz, h * 384, [[1, P], [1, 256]])).then_inc(ld_bias, 16)
            with sp.Fori(4, 6) as U:
                body(U, -512, -512)
            body(6, -512, -512, w2=False)

            def load_out(j):
                k = OUT_TILES[j]
                sp.dma_start(wo_raw[j % 4], w_out[0, k * P:(k + 1) * P, :]).then_inc(ld_wo[j % 4], 16)

            sp.wait_ge(wlo_ok, 31)
            load_out(0)
            sp.wait_ge(wlo_ok, 32)
            load_out(1)
            sp.wait_ge(tg_done, n(Unit(SB_UNITS, False).tg))
            load_out(2)
            sp.wait_ge(kl_ok, 16)
            sp.wait_ge(ql_ok, 16)
            sp.wait_ge(st_gate, 16)
            sp.dma_start(gate_b, gate_dram.ap().to_broadcast([P, D])).then_inc(ld_gate, 16)
            sp.wait_ge(bias_ok, 4)
            load_out(3)
            for j in range(4, KT):
                sp.wait_ge(wo_lo_pool if j - 4 in LO_POOL else wo_lo_dve, max(1, j - 4))
                load_out(j)
            for q, i in enumerate(ORDER):
                if q == 1:
                    sp.wait_ge(tg_done, n(Unit(7, False).tg + 2))
                if q >= 2:
                    sp.wait_ge(part_ok, 2 * q - 2)
                sp.dma_start(x_res[q % 2], x[0, i * P:(i + 1) * P, :]).then_inc(ld_xr[q % 2], 16)
                if q == 1:
                    sp.wait_ge(sg_ok, 8)
                    sp.dma_start(final_b, final_g.rearrange("(a n) -> a n", a=1).to_broadcast([P, D])).then_inc(ld_fg, 16)
            for q, i in enumerate(ORDER):
                sp.wait_ge(f_ok, q + 1)
                sp.dma_start(out[0, i * P:(i + 1) * P, :], out_ring[q % 4]).then_inc(st_out[q % 4], 16)
            for j in range(4):
                sp.wait_ge(st_out[j], 16 * NB // 4)

        @block.gpsimd
        def _(pool):
            g = nc.gpsimd
            g.memset(ident[:], 0.0).then_inc(consts, 1)
            g.memset(mask_bf[:], 0.0).then_inc(consts, 1)
            g.memset(half, -0.5).then_inc(consts, 1)
            pool.wait_ge(consts, 3)
            g.affine_select(out=ident[:], in_=ident[:], compare_op=ALU.not_equal, fill=1.0, base=0,
                            pattern=[[-1, P]], channel_multiplier=1).then_inc(ident_ok, 1)
            g.affine_select(out=mask_bf[:], in_=mask_bf[:], compare_op=ALU.is_gt, fill=NEG, base=0,
                            pattern=[[-1, P]], channel_multiplier=1).then_inc(ident_ok, 1)

            def split_lo(j, t):
                pool.wait_ge(whi_ok, j + 1)
                g.tensor_tensor(w_lo[:, t % 2], w_raw[:, t % 2], w_hi[:, t % 2], ALU.subtract).then_inc(wlo_ok, 1)

            for b in range(NB):
                pool.wait_ge(x_ms, b + 1)
                g.tensor_tensor(rstd[:, b:b + 1], ms[:, b:b + 1], half, ALU.pow).then_inc(x_rs, 1)
            for t in range(5):
                split_lo(t, t % 4)

            def body(U, sbk, w1=True, w2=True):
                un = Unit(U, sbk)
                ready = split_points(w1, w2)
                for t in range(SB_SLOTS if sbk else DA_SLOTS):
                    if not sbk and t % 2 == 0 and 6 <= t:
                        b = (t - 6) // 2
                        pool.wait_ge(ms_ok, 8 * un.da + b + 1)
                        g.tensor_tensor(rstd[:, b:b + 1], ms[:, b:b + 1], half, ALU.pow).then_inc(rstd_ok, 1)
                    for j in ready.get(t, ()):
                        split_lo(4 * U + 4 + j, j % 4)
                    if not w1:
                        if t < 2:
                            out_lo(LO_POOL[t])
                        if t % 2 and t < CHUNKS:
                            mixed_lo(t // 2)

            def out_lo(j):
                k = OUT_TILES[j]
                pool.wait_ge(wo_hi, j + 1)
                g.tensor_tensor(h_lo[:, k, :], wo_raw[j % 4], h_hi[:, k, :], ALU.subtract).then_inc(wo_lo_pool, 1)

            def mixed_lo(q):
                pool.wait_ge(mh_ok, q + 1)
                g.tensor_tensor(w_lo[:, q % 2], mixed_block(ORDER[q]), w_hi[:, q % 2], ALU.subtract).then_inc(ml_ok, 1)

            with pool.Fori(0, SB_UNITS) as U:
                body(U, True)
            with pool.Fori(4, 6) as U:
                body(U, False)
            body(6, False, w2=False)
            body(7, False, False, False)
            for q in range(NB):
                pool.wait_ge(f_sq, q + 1)
                g.tensor_scalar(ms[:, q:q + 1], sum_sq[:, q:q + 1], 1.0 / D, EPS, ALU.mult, ALU.add).then_inc(f_ms, 1)
                pool.wait_ge(f_ms, q + 1)
                g.tensor_tensor(rstd[:, q:q + 1], ms[:, q:q + 1], half, ALU.pow).then_inc(f_rs, 1)

        @block.scalar
        def _(act):
            s = nc.scalar
            for sem_ in (p_free, z_free, tg_free):
                act.sem_inc(sem_, 1)
            for row, src in ((0, c), (8, norm_g), (16, b_ada[:, 0:2 * D]), (32, subln_g)):
                src = src.rearrange("a (k p) -> (a k) p", p=P)
                act.dma_start(sq_sb[row:row + src.shape[0], :], src).then_inc(ld_small, 16)
            for j, v in enumerate((lq1, lk1, lq2, lk2)):
                act.dma_start(sg[:, j * HD:(j + 1) * HD], v.to_broadcast([P, HD])).then_inc(ld_lam, 16)
            with nc.allow_non_contiguous_dma(reason="a table of 4 x 32 values"):
                act.dma_start(rb[:, :], rel_bias.rearrange("b h -> h b")).then_inc(ld_rb, 16)
            act.wait_ge(col_ok, 1)
            s.activation(sc_col, c_col, ACT.Sigmoid).then_inc(sig_c, 1)
            for b in range(NB):
                act.wait_ge(ld_x[b % 4], 16 * (b // 4 + 1))
                if b:
                    act.wait_ge(x_sq, b)
                s.activation(vv[:].rearrange("p a b -> p (a b)"), st[:, b % 4, :], ACT.Square,
                             accum_out=sum_sq[:, b:b + 1]).then_inc(x_sq, 1)
                if b:
                    x_evac(act, b - 1)
            x_evac(act, NB - 1)
            act.wait_ge(lam_ok, 2)
            s.activation(lam_exp, lam_dot, ACT.Exp).then_inc(sig_c, 1)
            act.wait_ge(mod_ok, 1)
            act.wait_ge(xt_free, 2 * NB)
            for k in range(KT):
                s.activation(h_hi[:, k, :], mixed[:, k * S:(k + 1) * S], ACT.Identity,
                             bias=mod_col[:, k:k + 1], scale=a_col[:, k:k + 1]).then_inc(h_hi_ok, 1)

            def p_evac(U1, t, c_, st_free, bank=None):
                act.wait_ge(p_done, n(8 * U1 + 2 * t + c_ + 1))
                for sem_, v in st_free:
                    act.wait_ge(sem_, v)
                s.activation(st[:, t, c_ * 512:(c_ + 1) * 512], pp[:] if bank is None else bank, ACT.Copy,
                             scale=HD ** -0.5 if t == Q_ else 1.0).then_inc(p_free, 1)

            def commit(U):
                act.wait_ge(qk_done, n(16 * U))
                act.wait_ge(p_free, n(8 * U + 4))
                s.activation(kh[0:HD, 0, :], st[0:HD, K_, :], ACT.Copy).then_inc(kh_ok, 1)
                s.activation(kh[HD:P, 1, :], st[HD:P, K_, :], ACT.Copy).then_inc(kh_ok, 1)
                s.activation(qs[0:HD, 0, :], st[0:HD, Q_, :], ACT.Copy).then_inc(qh_ok, 1)
                s.activation(qs[HD:P, 1, :], st[HD:P, Q_, :], ACT.Copy).then_inc(qh_ok, 1)

            for t in range(4):
                for c_ in range(2):
                    p_evac(0, t, c_, ((xt_done, 2 * NB),), chunk_bank(t, c_))
                if t == 1:
                    commit(0)

            def t_evac(un, index, dst, j0, cnt, wait=()):
                act.wait_ge(tg_done, n(un.tg + index + 1))
                for sem_, v in wait:
                    act.wait_ge(sem_, v)
                s.activation(dst[:, j0 * P:(j0 + cnt) * P], tp[index % 2][:, 0:cnt, :].rearrange("p a b -> p (a b)"),
                             ACT.Copy).then_inc(tg_free, 1)

            def body(U, sbk, w1=True):
                un = Unit(U, sbk)
                vflat = vv[:].rearrange("p a b -> p (a b)")

                def evac_next(pieces):
                    for t, c_ in groups_ending(pieces):
                        free = {K_: ((kl_ok, 2 * U + 2),), Q_: ((ql_ok, 2 * U + 2),),
                                V_: ((tg_done, n(un.tg + 2)),), G_: ((sg_ok, U + 1),)}[t]
                        p_evac(U + 1, t, c_, free)

                if not w1:
                    for j in range(3):
                        out_hi(j)
                t_evac(un, 0, vflat, 0, 4, ((pv_done, n(un.w)),))
                t_evac(un, 1, vflat, 4, 4)
                if w1:
                    evac_next(range(HEAD_PIECES))
                else:
                    out_hi(3)
                for t in range(SB_SLOTS if sbk else DA_SLOTS):
                    if t < 16:
                        i, m = STEPS[t]
                        L = (i + 1) * P
                        if sbk:
                            act.wait_ge(qk_done, n(un.qk + t + 1))
                            act.wait_ge(tg_done, n(un.transposed(t - 2) if t >= 3 else un.tg))
                            s.activation(prob[t % 3][:, 0:L], z[t % 2][:, 0:L], ACT.Sigmoid,
                                         scale=-1.0).then_inc(keep_ok, 1)
                            act.wait_ge(w_ok, n(un.w + (t - 1 if t >= 2 else 0)))
                            s.activation(beta[t % 2][:, 0:L], z[t % 2][:, 0:L], ACT.Sigmoid).then_inc(z_free, 1)
                        else:
                            b = t // 2
                            act.wait_ge(max_ok, 16 * un.da + t + 1)
                            if m == 0:
                                act.wait_ge(tg_done, n(un.transposed(b - 1) if b >= 2 else un.tg))
                            else:
                                act.wait_ge(w_ok, n(un.w + (b - 1 if b >= 2 else 0)))
                            dst = prob[b % 2] if m == 0 else beta[b % 2]
                            s.activation(dst[:, 0:L], z[t % 2][:, 0:L], ACT.Exp, bias=neg_max[:, t:t + 1],
                                         accum_out=row_sum[:, t:t + 1]).then_inc(z_free, 1)
                    if not w1:
                        for j in {0: (4, 5), 1: (6,), 3: (7,)}.get(t, ()):
                            out_hi(j)
                    if t == 16 and w1:
                        commit(U + 1)
                    if sbk and 2 <= t < 18:
                        evac_step(un, t - 2, STEPS[t - 2][0], sb_tgroups_before(t - 2))
                    if not sbk and t >= 3 and t % 2 and t < 18:
                        b = (t - 3) // 2
                        evac_step(un, b, ORDER[b], da_tgroups_before(b))
                    if w1:
                        evac_next(pieces_of_slot(t, sbk))
                    if t == (1 if sbk else 2):
                        act.wait_ge(mixed_ok, n(un.mixed))
                        act.wait_ge(p_free, n(8 * U + 8))
                        s.activation(sg[:], st[:, G_, :], ACT.Sigmoid).then_inc(sg_sig, 1)

            def out_hi(j):
                k = OUT_TILES[j]
                if k == LAST:
                    act.wait_ge(last_gated, 1)
                else:
                    act.wait_ge(ld_wo[j % 4], 16 * (j // 4 + 1))
                if j == 0:
                    act.wait_ge(p_done, n(64))
                s.activation(h_hi[:, k, :], wo_raw[j % 4], ACT.Copy).then_inc(wo_hi, 1)

            def evac_step(un, k, i, g0):
                wait = ((pv_done, n(un.w + (k - 1 if k >= 2 else 0))),)
                for gidx, j0 in enumerate(range(0, i + 1, 4)):
                    t_evac(un, g0 + gidx, wT[k % 2], j0, min(4, i + 1 - j0), wait)

            act.wait_ge(st_gate, 16)
            with act.Fori(0, SB_UNITS) as U:
                body(U, True)
            with act.Fori(4, 7) as U:
                body(U, False)
            body(7, False, False)

            for q in range(NB):
                act.wait_ge(r_ok, q + 1)
                if q:
                    act.wait_ge(f_sq, q)
                else:
                    act.wait_ge(pv_done, n(96))
                s.activation(wT[0].rearrange("p (k n) -> p k n", k=KT), mixed_block(ORDER[q]), ACT.Square,
                             accum_out=sum_sq[:, q:q + 1]).then_inc(f_sq, 1)

        @block.vector
        def _(dve):
            v = nc.vector
            for sem_ in (mixed_ok, w_ok):
                dve.sem_inc(sem_, 1)
            chain = [0]

            def link(ins):
                chain[0] += 1
                ins.then_inc(dve_pro, 1)
                dve.wait_ge(dve_pro, chain[0])

            dve.wait_ge(ident_ok, 1)
            v.tensor_copy(ident_r[:], ident[:]).then_inc(sc_ok, 1)
            v.tensor_copy(ident_bf[:], ident[:]).then_inc(sc_ok, 1)
            v.memset(ones_col, 1.0).then_inc(sc_ok, 1)
            dve.wait_ge(col_t, 1)
            v.tensor_copy(raw_col, pp[:, 0:33]).then_inc(col_ok, 1)
            dve.wait_ge(sig_c, 1)
            v.tensor_tensor(sc_col, sc_col, c_col, ALU.mult).then_inc(sc_ok, 1)
            v.tensor_scalar(gs_col, sub_col, 1.0 - LAMBDA_INIT, None, ALU.mult).then_inc(sc_ok, 1)
            dve.wait_ge(sc_ok, 4)

            def scale_x(b):
                dve.wait_ge(x_sq, b + 1)
                v.tensor_scalar(ms[:, b:b + 1], sum_sq[:, b:b + 1], 1.0 / D, EPS, ALU.mult, ALU.add).then_inc(x_ms, 1)
                dve.wait_ge(x_rs, b + 1)
                v.tensor_scalar(st[:, b % 4, :], st[:, b % 4, :], rstd[:, b:b + 1], None, ALU.mult).then_inc(x_scaled, 1)

            def add_ada(j):
                k = j % KT
                acc, tile = ada_sum[:, j // KT % 2 * D:(j // KT % 2 + 1) * D], work[:, j % 6 * D:(j % 6 + 1) * D]
                dve.wait_ge(ld_ada[j % 6], 16 * (j // 6 + 1))
                if k == 0:
                    v.tensor_scalar(acc, tile, sc_col[:, k:k + 1], None, ALU.mult).then_inc(ada_used, 1)
                else:
                    dve.wait_ge(ada_used, j)
                    v.scalar_tensor_tensor(acc, tile, sc_col[:, k:k + 1], acc, ALU.mult, ALU.add).then_inc(ada_used, 1)

            for b in range(NB):
                if b == 4:
                    for j in range(4):
                        add_ada(j)
                scale_x(b)
            for h in range(2):
                if h == 1:
                    dve.wait_ge(ld_lam, 64)
                    for j in range(2):
                        v.tensor_tensor(sg[:, 256 + j * HD:256 + (j + 1) * HD], sg[:, 2 * j * HD:(2 * j + 1) * HD],
                                        sg[:, (2 * j + 1) * HD:(2 * j + 2) * HD], ALU.mult).then_inc(dve_pro, 1)
                    chain[0] += 2
                    dve.wait_ge(dve_pro, chain[0])
                    v.tensor_reduce(lam_dot, sg[:, 256:256 + 2 * HD].rearrange("p (a b) -> p a b", a=2), AX.X,
                                    ALU.add).then_inc(lam_ok, 2)
                for j in range(KT * h if h else 4, KT * h + KT):
                    add_ada(j)
            dve.wait_ge(sig_c, 2)
            link(v.tensor_scalar(lam_tmp, lam_exp[:, 1:2], -LAMBDA_INIT, None, ALU.add))
            link(v.tensor_tensor(nlam, lam_tmp, lam_exp[:, 0:1], ALU.subtract))
            for t in range(2):
                dve.wait_ge(ld_w[t], 16)
                v.tensor_copy(w_hi[:, t], w_raw[:, t]).then_inc(whi_ok, 1)
            dve.wait_ge(mod_mm, 2)
            link(v.tensor_tensor(mod_col, z[0][:, 0:16], b_col, ALU.add))
            v.scalar_tensor_tensor(a_col, mod_col[:, 8:16], 1.0, g_col, ALU.add, ALU.mult).then_inc(mod_ok, 1)
            dve.wait_ge(mod_ok, 1)

            def commit_k(U):
                dve.wait_ge(kh_ok, 2 * U + 2)
                v.tensor_tensor(kl[0:HD, 0, :], st[0:HD, K_, :], kh[0:HD, 0, :], ALU.subtract).then_inc(kl_ok, 1)
                v.tensor_tensor(kl[HD:P, 1, :], st[HD:P, K_, :], kh[HD:P, 1, :], ALU.subtract).then_inc(kl_ok, 1)

            def commit_q(U):
                dve.wait_ge(qh_ok, 2 * U + 2)
                v.tensor_tensor(qs[HD:P, 0, :], st[0:HD, Q_, :], qs[0:HD, 0, :], ALU.subtract).then_inc(ql_ok, 1)
                v.tensor_tensor(qs[0:HD, 1, :], st[HD:P, Q_, :], qs[HD:P, 1, :], ALU.subtract).then_inc(ql_ok, 1)

            def split_hi(U1, t):
                dve.wait_ge(ld_w[t % 2], 32 * U1 + 16 * (t // 2 + 1))
                dve.wait_ge(p_done, n(8 * U1 + 2 * t - 2))
                v.tensor_copy(w_hi[:, t % 2], w_raw[:, t % 2]).then_inc(whi_ok, 1)

            for k in range(KT):
                xk = mixed[:, k * S:(k + 1) * S]
                dve.wait_ge(h_hi_ok, k + 1)
                link(v.tensor_scalar(xk, xk, a_col[:, k:k + 1], mod_col[:, k:k + 1], ALU.mult, ALU.add))
                v.tensor_tensor(h_lo[:, k, :], xk, h_hi[:, k, :], ALU.subtract).then_inc(h_ok, 1)
            for t in range(2, 4):
                split_hi(0, t)
            for j in range(2 * KT, 3 * KT):
                if j == 2 * KT + 3:
                    commit_k(0)
                    commit_q(0)
                add_ada(j)
            split_hi(1, 0)
            dve.wait_ge(gate_mm, 1)
            dve.wait_ge(ld_bg, 16)
            v.tensor_tensor(sg[0:1, :], z[0][0:1, :], sg[0:1, :], ALU.add).then_inc(gate_row, 1)
            dve.wait_ge(ld_rb, 16)
            link(v.tensor_scalar(rb[:, :], rb[:, :], rb[:, N_BUCKETS - 1:N_BUCKETS], None, ALU.subtract))
            link(v.memset(rv[:, 0:P - 1], NEG))
            for bkt, (lo, hi) in enumerate(buckets_by_distance()):
                fill = v.tensor_copy(rv[:, P - 1 + lo:P + hi], rb[:, bkt:bkt + 1].to_broadcast([4, hi - lo + 1]))
                if bkt < N_BUCKETS - 1:
                    link(fill)
            fill.then_inc(rv_ok, 1)
            v.memset(stick[:, :], 1.0).then_inc(dve_pro, 1)
            chain[0] += 1
            dve.wait_ge(dve_pro, chain[0])

            def body(U, sbk, w1=True, w2=True):
                un = Unit(U, sbk)
                ready = split_points(w1, w2)

                def splits(t):
                    for j in ready.get(t, ()):
                        split_hi(U + 1 + j // 4, j % 4)
                    if not w1:
                        last_unit_work(t)

                def gated(b):
                    i = ORDER[b]
                    dve.wait_ge(sg_ok, U + 1)
                    gate = sg[:, i * P:(i + 1) * P]
                    if sbk:
                        dve.wait_ge(pv_done, n(un.w + 2 * b + 2))
                        v.tensor_tensor(mixed[:, bass.ds((U + 4) * S + i * P, P)], oo[:, 0:P], gate,
                                        ALU.mult).then_inc(mixed_ok, 1)
                    else:
                        dve.wait_ge(ot_done, n(8 * un.da + b + 1))
                        dst = mixed[:, bass.ds((U - 4) * S + i * P, P)] if w1 else last_out[:, i * P:(i + 1) * P]
                        if not w1 and b == 0:
                            dve.wait_ge(wo_lo_dve, 5)
                        v.scalar_tensor_tensor(dst, oo[:, P:2 * P], gs_col, gate, ALU.mult, ALU.mult).then_inc(mixed_ok, 1)

                if not sbk:
                    dve.wait_ge(qk_done, n(un.qk))
                    dve.wait_ge(ld_bias, 64)
                    braw = stick[:, bass.ds(un.da * 256, 256)]
                    v.tensor_copy(bias_hi[:, ::-1], braw).then_inc(bias_hi_ok, 1)
                    dve.wait_ge(bias_hi_ok, un.da + 1)
                    v.tensor_tensor(bias_lo[:, ::-1], braw, bias_hi[:, ::-1], ALU.subtract).then_inc(bias_ok, 1)
                splits(-1)
                for t in range(SB_SLOTS if sbk else DA_SLOTS):
                    L = (STEPS[t][0] + 1) * P if t < 16 else 0
                    if not w1 and 0 <= t - 1 - FIRST_CHUNK < CHUNKS:
                        partial(t - 1 - FIRST_CHUNK)
                    if not w1 and t % 2 and t >= 7:
                        gated((t - 7) // 2)
                    if not w1 and t % 2 and t < CHUNKS:
                        mixed_hi(t // 2)
                    if sbk:
                        if t >= 5 and t % 2:
                            gated((t - 5) // 2)
                        if t < 16:
                            dve.wait_ge(keep_ok, un.qk + t + 1)
                            dve.wait_ge(w_ok, n(un.w + t))
                            kp = prob[t % 3][:, 0:L][:, ::-1]
                            v.tensor_tensor_scan(stick[:, 0:L][:, ::-1], kp, kp, 1.0,
                                                 ALU.mult, ALU.bypass).then_inc(scan_ok, 1)
                        if t < 16:
                            dve.wait_ge(z_free, n(un.qk + t + 1))
                            dve.wait_ge(scan_ok, un.qk + t + 1)
                            v.tensor_tensor(prob[t % 3][:, 0:L], beta[t % 2][:, 0:L], stick[:, 1:L + 1],
                                            ALU.mult).then_inc(w_ok, 1)
                    else:
                        leaves = t % 2 == 0 and 6 <= t
                        if leaves:
                            da_leave_1(un, (t - 6) // 2)
                        if t < 16:
                            dve.wait_ge(qk_done, n(un.qk + t + 1))
                            v.tensor_reduce(neg_max[:, t:t + 1], z[t % 2][:, 0:L], AX.X, ALU.max,
                                            negate=True).then_inc(max_ok, 1)
                        if leaves:
                            da_leave_2(un, (t - 6) // 2)
                        if t >= 2 and t % 2 == 0 and t <= 16:
                            combine(un, t // 2 - 1)
                        if not w1 and t == DA_SLOTS - 1:
                            result(0)
                            result(1)
                        if leaves and (w1 or t == DA_SLOTS - 1):
                            gated((t - 6) // 2)
                    if t == (3 if sbk else 4):
                        dve.wait_ge(sg_sig, U + 1)
                        v.tensor_tensor(sg[:], sg[:], st[:, G_, :], ALU.mult).then_inc(sg_ok, 1)
                    if t == 16 and w1:
                        commit_k(U + 1)
                    if t == (16 if sbk else 18) and w1:
                        commit_q(U + 1)
                    splits(t)

            def last_unit_work(t):
                if t == 3:
                    dve.wait_ge(ld_wo[3], 32)
                    dve.wait_ge(ld_gate, 16)
                    v.tensor_tensor(wo_raw[3], wo_raw[3], gate_b, ALU.mult).then_inc(last_gated, 1)
                for j in {-1: (1,), 0: (2, 3), 1: (5,), 2: (6,), 4: (7,)}.get(t, ()):
                    dve.wait_ge(wo_hi, j + 1)
                    v.tensor_tensor(h_lo[:, OUT_TILES[j], :], wo_raw[j % 4], h_hi[:, OUT_TILES[j], :],
                                    ALU.subtract).then_inc(wo_lo_dve, 1)
                if t in (17, 19, 20):
                    lo, hi, i = {17: (2 * P, S, 0), 19: (P, 2 * P, 1), 20: (0, P, 2)}[t]
                    dve.wait_ge(qk_done, n(128))
                    dve.wait_ge(mixed_ok, n(62 + i))
                    v.tensor_copy(last_hi[:, lo:hi], last_out[:, lo:hi]).then_inc(oh_ok, 1)
                    dve.wait_ge(oh_ok, i + 1)
                    v.tensor_tensor(last_lo[:, lo:hi], last_out[:, lo:hi], last_hi[:, lo:hi],
                                    ALU.subtract).then_inc(o_split, 1)

            def mixed_hi(q):
                dve.wait_ge(mixed_ok, n(56))
                if q >= 2:
                    dve.wait_ge(part_done, 2 * q - 2)
                else:
                    dve.wait_ge(p_done, n(64))
                v.tensor_copy(w_hi[:, q % 2], mixed_block(ORDER[q])).then_inc(mh_ok, 1)

            def partial(c):
                q, ch = c // 2, c % 2
                dst = mixed_block(ORDER[q])[:, 4 * ch:4 * ch + 4, :]
                cols_ = slice(ch * 512, (ch + 1) * 512)
                parts = lambda ap: ap.rearrange("p (k n) -> p k n", k=4)
                dve.wait_ge(part_done, c + 1)
                dve.wait_ge(ml_ok, q + 1)
                dve.wait_ge(ld_gate, 16)
                v.tensor_tensor(dst, parts(pp[:]), parts(gate_b[:, cols_]), ALU.mult).then_inc(part_free, 1)
                dve.wait_ge(part_free, c + 1)
                dve.wait_ge(ld_xr[q % 2], 16 * (q // 2 + 1))
                v.tensor_tensor(dst, dst, parts(x_res[q % 2][:, cols_]), ALU.add).then_inc(part_ok, 1)

            def result(q):
                dve.wait_ge(y_done, q + 1)
                dve.wait_ge(part_ok, 2 * q + 2)
                v.tensor_tensor(mixed_block(ORDER[q]), z[q % 2][:].rearrange("p (k n) -> p k n", k=KT),
                                mixed_block(ORDER[q]), ALU.add).then_inc(r_ok, 1)

            def combine(un, b):
                i = ORDER[b]
                L = (i + 1) * P
                t0 = 2 * b
                dve.wait_ge(z_free, n(un.qk + t0 + 2))
                v.reciprocal(inv_sum[:, t0:t0 + 2], row_sum[:, t0:t0 + 2]).then_inc(inv_ok, 1)
                dve.wait_ge(inv_ok, 8 * un.da + b + 1)
                v.tensor_scalar(ratio[:, b:b + 1], row_sum[:, t0:t0 + 1], inv_sum[:, t0 + 1:t0 + 2], nlam,
                                ALU.mult, ALU.mult).then_inc(ratio_ok, 1)
                dve.wait_ge(ratio_ok, 8 * un.da + b + 1)
                v.scalar_tensor_tensor(prob[b % 2][:, 0:L], beta[b % 2][:, 0:L], ratio[:, b:b + 1],
                                       prob[b % 2][:, 0:L], ALU.mult, ALU.add).then_inc(w_ok, 1)

            def da_leave_1(un, b):
                dve.wait_ge(pv_done, n(un.w + b + 1))
                dve.wait_ge(ot_done, n(8 * un.da + b))
                v.tensor_scalar(o_sb[:], oo[:, 0:P], inv_sum[:, 2 * b:2 * b + 1], None, ALU.mult).then_inc(onorm_ok, 1)
                dve.wait_ge(onorm_ok, 8 * un.da + b + 1)
                v.tensor_tensor(sq_sb[:], o_sb[:], o_sb[:], ALU.mult).then_inc(sq_ok, 1)
                dve.wait_ge(sq_ok, 8 * un.da + b + 1)
                v.tensor_reduce(sum_sq[:, b:b + 1], sq_sb[:], AX.X, ALU.add).then_inc(ssq_ok, 1)
                dve.wait_ge(ssq_ok, 8 * un.da + b + 1)
                v.tensor_scalar(ms[:, b:b + 1], sum_sq[:, b:b + 1], 1.0 / P, EPS, ALU.mult, ALU.add).then_inc(ms_ok, 1)

            def da_leave_2(un, b):
                dve.wait_ge(rstd_ok, 8 * un.da + b + 1)
                v.tensor_scalar(o_sb[:], o_sb[:], rstd[:, b:b + 1], None, ALU.mult).then_inc(o_ok, 1)

            with dve.Fori(0, SB_UNITS) as U:
                body(U, True)
            with dve.Fori(4, 6) as U:
                body(U, False)
            body(6, False, w2=False)
            body(7, False, False, False)

            def final_scale(q):
                dve.wait_ge(f_rs, q + 1)
                if q >= 4:
                    dve.wait_ge(st_out[q % 4], 16)
                parts = lambda ap: ap.rearrange("p (k n) -> p k n", k=KT)
                v.scalar_tensor_tensor(parts(out_ring[q % 4]), mixed_block(ORDER[q]), rstd[:, q:q + 1], parts(final_b),
                                       ALU.mult, ALU.mult).then_inc(f_ok, 1)

            dve.wait_ge(ld_fg, 16)
            dve.wait_ge(tg_done, n(Unit(UNITS, False).tg))
            for q in range(2, NB):
                result(q)
                final_scale(q - 2)
            final_scale(NB - 2)
            final_scale(NB - 1)

        @block.tensor
        def _(pe):
            t_ = nc.tensor
            for sem_ in (p_done, qk_done, tg_done, pv_done, ot_done):
                pe.sem_inc(sem_, 1)

            def transpose_x(b):
                pe.wait_ge(x_scaled, b + 1)
                for gidx in range(2):
                    if b:
                        pe.wait_ge(xt_free, 2 * b + gidx - 1)
                    for j in range(4):
                        k = 4 * gidx + j
                        tr = t_.transpose(tp[gidx][:, j, :], st[:, b % 4, k * P:(k + 1) * P], ident[:])
                    tr.then_inc(xt_done, 1)

            pe.wait_ge(ident_ok, 2)
            pe.wait_ge(ld_small, 64)
            t_.transpose(pp[:, 0:33], sq_sb[0:33, :], ident[0:33, 0:33]).then_inc(col_t, 1)
            pe.wait_ge(sc_ok, 4)
            for b in range(NB):
                transpose_x(b)
            for h in range(2):
                pe.wait_ge(ada_used, KT * (h + 1))
                for j in range(KT * h, KT * h + KT):
                    mm = t_.matmul(z[0][:, j:j + 1], ada_sum[:, j * P:(j + 1) * P], ones_col,
                                   start=j == 0, stop=True, skip_group_check=True)
                mm.then_inc(mod_mm, 1)

            def piece(U1, p, first=False, bank=None):
                t, c_, pas = p // 6, p % 6 // 3, p % 3
                if p % 6 == 0:
                    pe.wait_ge(whi_ok, 4 * U1 + t + 1)
                if p % 6 == 2:
                    pe.wait_ge(wlo_ok, 4 * U1 + t + 1)
                if bank is not None and pas == 0:
                    pe.wait_ge(p_free, n(t + 1))
                elif pas == 0 and not first:
                    pe.wait_ge(p_free, n(8 * U1 + 2 * t + c_))
                lhs = w_lo if pas == 2 else w_hi
                rhs = h_lo if pas == 1 else h_hi
                for k in range(KT):
                    mm = t_.matmul(pp[:] if bank is None else bank, lhs[:, t % 2, k, :],
                                   rhs[:, k, c_ * 512:(c_ + 1) * 512],
                                   start=(pas == 0 and k == 0), stop=(pas == 2 and k == KT - 1))
                if pas == 2:
                    mm.then_inc(p_done, 1)

            pe.wait_ge(wlo_ok, 2)
            for k in range(KT):
                pe.wait_ge(h_ok, k + 1)
                for t in range(2):
                    for c_ in range(2):
                        for pas in range(3):
                            mm = t_.matmul(z[t][:, c_ * 512:(c_ + 1) * 512], (w_lo if pas == 2 else w_hi)[:, t, k, :],
                                           (h_lo if pas == 1 else h_hi)[:, k, c_ * 512:(c_ + 1) * 512],
                                           start=(pas == 0 and k == 0), stop=(pas == 2 and k == KT - 1))
                        if k == KT - 1:
                            mm.then_inc(p_done, 1)
            for p in range(12, PIECES):
                t, c_ = p // 6, p % 6 // 3
                piece(0, p, p == 12, chunk_bank(t, c_) if c_ else None)
                if p == 20:
                    pe.wait_ge(ada_used, 3 * KT)
                    pe.wait_ge(p_free, n(2))
                    for ch in range(2):
                        mm = t_.matmul(z[0][0:1, ch * 512:(ch + 1) * 512], ones_col,
                                       ada_sum[:, ch * 512:(ch + 1) * 512], start=True, stop=True)
                    mm.then_inc(gate_mm, 1)
            pe.wait_ge(gate_row, 1)

            def logits(un, t):
                i, m = STEPS[t]
                L = (i + 1) * P
                pe.wait_ge(z_free, n(un.qk + (t - 1 if t >= 2 else 0)))
                for ch in range(0, L, 512):
                    e = min(ch + 512, L)
                    q = qs[:, m, i * P:(i + 1) * P]
                    if un.sb:
                        adds = [(ident_bf, mask_bf, i * P, (i + 1) * P, 0)]
                    else:
                        adds = [(ident_r, bb, lo, hi, (1 - i) * P) for bb in (bias_hi, bias_lo)
                                for lo, hi in [(max(i - 1, 0) * P, (i + 1) * P)]]
                    adds = [(a, bb, max(lo, ch), min(hi, e), off) for a, bb, lo, hi, off in adds if max(lo, ch) < min(hi, e)]
                    t_.matmul(z[t % 2][:, ch:e], q, kh[:, m, ch:e], start=True, stop=False)
                    mm = t_.matmul(z[t % 2][:, ch:e], q, kl[:, m, ch:e], start=False, stop=not adds)
                    for x_, (a, bb, lo, hi, off) in enumerate(adds):
                        if un.sb:
                            mm = t_.matmul(z[t % 2][:, lo:hi], a[:], bb[:], start=False, stop=True)
                        else:
                            mm = t_.matmul(z[t % 2][:, lo:hi], a[:], bb[:, lo + off:hi + off], start=False,
                                           stop=x_ == len(adds) - 1)
                mm.then_inc(qk_done, 1)

            def transposes(un, k, i, src, g0):
                pe.wait_ge(w_ok, n(un.w + k + 1))
                for gidx, j0 in enumerate(range(0, i + 1, 4)):
                    pe.wait_ge(tg_free, n(un.tg + g0 + gidx - 1))
                    for j in range(j0, min(j0 + 4, i + 1)):
                        tr = t_.transpose(tp[(g0 + gidx) % 2][:, j - j0, :], src[:, j * P:(j + 1) * P], ident[:])
                    tr.then_inc(tg_done, 1)

            def values(un, k, i, b, m):
                pe.wait_ge(tg_free, n(un.transposed(k + 1)))
                if not m:
                    pe.wait_ge(mixed_ok, n(un.mixed + b))
                for j in range(i + 1):
                    wt = wT[k % 2][:, j * P:(j + 1) * P]
                    if m is None:
                        mm = t_.matmul(oo[:, 0:P], wt, vv[:, j, :], start=j == 0, stop=j == i)
                    else:
                        mm = t_.matmul(oo[m * HD:(m + 1) * HD, 0:P], vv[:, j, m * HD:(m + 1) * HD], wt,
                                       start=j == 0, stop=j == i)
                mm.then_inc(pv_done, 1)

            def body(U, sbk, w1=True):
                un = Unit(U, sbk)
                pe.wait_ge(p_free, n(8 * U + 6))
                for gidx in range(2):
                    pe.wait_ge(tg_free, n(un.tg))
                    for j in range(4):
                        tr = t_.transpose(tp[gidx][:, j, :], st[:, V_, (4 * gidx + j) * P:(4 * gidx + j + 1) * P], ident[:])
                    tr.then_inc(tg_done, 1)
                if w1:
                    for p in range(HEAD_PIECES):
                        piece(U + 1, p)
                pe.wait_ge(ql_ok, 2 * U + 2)
                pe.wait_ge(dup_ok, 64 * U + 64)
                pe.wait_ge(kl_ok, 2 * U + 2)
                if not sbk:
                    pe.wait_ge(bias_ok, un.da + 1)
                for t in range(SB_SLOTS if sbk else DA_SLOTS):
                    if t < 16:
                        logits(un, t)
                    if sbk and 2 <= t < 18:
                        transposes(un, t - 2, STEPS[t - 2][0], prob[(t - 2) % 3], sb_tgroups_before(t - 2))
                    if not w1 and 0 <= t - FIRST_CHUNK < CHUNKS:
                        partial(t - FIRST_CHUNK)
                    if not w1 and t == DA_SLOTS - 1:
                        output(0)
                        output(1)
                    ps = list(pieces_of_slot(t, sbk)) if w1 else []
                    for p in ps[:1]:
                        piece(U + 1, p)
                    for p in ps[1:]:
                        piece(U + 1, p)
                    if not sbk and t % 2 == 0 and 6 <= t:
                        b = (t - 6) // 2
                        pe.wait_ge(o_ok, 8 * un.da + b + 1)
                        t_.transpose(oo[:, P:2 * P], o_sb[:], ident[:]).then_inc(ot_done, 1)
                    if sbk and 3 <= t < 19:
                        values(un, t - 3, STEPS[t - 3][0], (t - 3) // 2, (t - 3) % 2)
                    if not sbk and t % 2 and 3 <= t < 18:
                        b = (t - 3) // 2
                        transposes(un, b, ORDER[b], prob[b % 2], da_tgroups_before(b))
                    if not sbk and t % 2 and 5 <= t < 20:
                        values(un, (t - 5) // 2, ORDER[(t - 5) // 2], (t - 5) // 2, None)

            def partial(c):
                q, ch = c // 2, c % 2
                if c == 0:
                    pe.wait_ge(p_free, n(64))
                    pe.wait_ge(wo_hi, KT - 1)
                    pe.wait_ge(wo_lo_pool, 2)
                    pe.wait_ge(wo_lo_dve, 5)
                else:
                    pe.wait_ge(part_free, c)
                if ch == 0:
                    pe.wait_ge(ml_ok, q + 1)
                for pas in range(3):
                    lhs, rhs = (w_lo if pas == 2 else w_hi), (h_lo if pas == 1 else h_hi)
                    for k in OUT_TILES[:-1]:
                        mm = t_.matmul(pp[:], lhs[:, q % 2, k, :], rhs[:, k, ch * 512:(ch + 1) * 512],
                                       start=(pas == 0 and k == 0), stop=(pas == 2 and k == KT - 1))
                mm.then_inc(part_done, 1)

            def output(q):
                i = ORDER[q]
                if q == 0:
                    pe.wait_ge(wo_hi, KT)
                    pe.wait_ge(wo_lo_dve, 6)
                    pe.wait_ge(z_free, n(128))
                pe.wait_ge(o_split, max(1, q - 4))
                if q >= 2:
                    pe.wait_ge(r_ok, q - 1)
                for ch in range(2):
                    for pas in range(3):
                        lhs, rhs = (last_lo if pas == 2 else last_hi), (h_lo if pas == 1 else h_hi)
                        mm = t_.matmul(z[q % 2][:, ch * 512:(ch + 1) * 512], lhs[:, i * P:(i + 1) * P],
                                       rhs[:, LAST, ch * 512:(ch + 1) * 512], start=pas == 0, stop=pas == 2)
                mm.then_inc(y_done, 1)

            with pe.Fori(0, SB_UNITS) as U:
                body(U, True)
            with pe.Fori(4, 7) as U:
                body(U, False)
            body(7, False, False)

            for q in range(2, NB):
                output(q)


_INS = ["x", "c", "norm_g", "w_ada", "b_ada", "w_in", "lambda_q1", "lambda_k1", "lambda_q2", "lambda_k2",
        "subln_g", "w_out", "rel_bias", "final_g"]


def kernel(**inputs):
    import numpy as _np
    import concourse.bacc as _bacc
    from concourse.bass_utils import run_bass_kernel_spmd as _run

    nc = _bacc.Bacc("TRN2", target_bir_lowering=False, num_devices=1)
    arrays, args = {}, []
    for name in _INS:
        a = _np.ascontiguousarray(inputs[name])
        arrays[f"in_{name}_dram"] = a
        args.append(nc.dram_tensor(f"in_{name}_dram", a.shape, mybir.dt.from_np(a.dtype), kind="ExternalInput").ap())
    out = nc.dram_tensor("out_0_dram", (1, S, D), F32, kind="ExternalOutput").ap()
    layer_kernel(nc, *args, out)
    r = _run(nc, [arrays], core_ids=[0])
    return r.results[0]["out_0_dram"]
```
